# Optimizing a Trainium2 kernel written in Bass

```python
import math
import jax, jax.numpy as jnp
from jax import lax
import numpy as np

D_MODEL = 1024
BATCH = 1
SEQ = 512
DEPTH = 2

N_MIXERS = 2
N_SSD_LAYERS = (DEPTH + 1) // 2
N_HGRN_LAYERS = DEPTH // 2

SSD_EXPAND = 2
SSD_D_INNER = SSD_EXPAND * D_MODEL
SSD_HEAD_DIM = 64
SSD_N_HEADS = SSD_D_INNER // SSD_HEAD_DIM
SSD_N_GROUPS = 4
SSD_HEADS_PER_GROUP = SSD_N_HEADS // SSD_N_GROUPS
SSD_D_STATE = 128
SSD_CONV_WIDTH = 4
SSD_CHUNK = 128
SSD_BC_DIM = SSD_N_GROUPS * SSD_D_STATE
SSD_CONV_DIM = SSD_D_INNER + 2 * SSD_BC_DIM
SSD_IN_DIM = SSD_D_INNER + SSD_CONV_DIM + SSD_N_HEADS

HGRN_EXPAND = 128
HGRN_N_HEADS = D_MODEL // HGRN_EXPAND
HGRN_HEAD_V = D_MODEL // HGRN_N_HEADS
HGRN_CHUNK = 64
HGRN_IN_DIM = 4 * D_MODEL

D_FF = 4 * D_MODEL
PLE_DIM = 256
DEEPNORM_ALPHA = (2.0 * DEPTH) ** 0.25
DEEPNORM_BETA = (8.0 * DEPTH) ** -0.25
LN_EPS = 1e-5
RMS_EPS = 1e-5


def layer_norm(x, g, b):
    xf = x.astype(jnp.float32)
    mu = jnp.mean(xf, axis=-1, keepdims=True)
    xc = xf - mu
    var = jnp.mean(xc * xc, axis=-1, keepdims=True)
    y = xc * lax.rsqrt(var + LN_EPS) * g.astype(jnp.float32) + b.astype(jnp.float32)
    return y.astype(x.dtype)

def rms_norm(x, w):
    xf = x.astype(jnp.float32)
    return xf * lax.rsqrt(jnp.mean(xf * xf, axis=-1, keepdims=True) + RMS_EPS) * w.astype(jnp.float32)

def causal_depthwise_conv(u, w, b):
    k, c = w.shape
    out = lax.conv_general_dilated(u, w[:, None, :].astype(u.dtype), window_strides=(1,),
                                   padding=[(k - 1, 0)], dimension_numbers=('NWC', 'WIO', 'NWC'),
                                   feature_group_count=c)
    return out + b

def segsum_exp(a):
    t = a.shape[-1]
    cs = jnp.cumsum(a, axis=-1)
    seg = cs[..., :, None] - cs[..., None, :]
    mask = jnp.tril(jnp.ones((t, t), dtype=bool))
    return jnp.exp(jnp.where(mask, seg, -jnp.inf))

def ssd_mixer(u, w_in, conv_w, conv_b, dt_bias, a_log, d_skip, norm_w, w_out):
    bsz, seq, _ = u.shape
    nc = seq // SSD_CHUNK
    g_, r_, p_, n_ = SSD_N_GROUPS, SSD_HEADS_PER_GROUP, SSD_HEAD_DIM, SSD_D_STATE
    zxbcdt = u @ w_in
    z, xbc, dt = jnp.split(zxbcdt, [SSD_D_INNER, SSD_D_INNER + SSD_CONV_DIM], axis=-1)
    xbc = jax.nn.silu(causal_depthwise_conv(xbc, conv_w, conv_b))
    xs, bm, cm = jnp.split(xbc, [SSD_D_INNER, SSD_D_INNER + SSD_BC_DIM], axis=-1)
    xs = xs.astype(jnp.float32).reshape(bsz, nc, SSD_CHUNK, g_, r_, p_)
    bm = bm.astype(jnp.float32).reshape(bsz, nc, SSD_CHUNK, g_, n_)
    cm = cm.astype(jnp.float32).reshape(bsz, nc, SSD_CHUNK, g_, n_)
    dt = jax.nn.softplus(dt.astype(jnp.float32) + dt_bias.astype(jnp.float32))
    a = -jnp.exp(a_log.astype(jnp.float32))
    dt = dt.reshape(bsz, nc, SSD_CHUNK, g_, r_)
    da = dt * a.reshape(g_, r_)
    xdt = xs * dt[..., None]
    a_cs = jnp.cumsum(da, axis=2)
    decay = segsum_exp(jnp.moveaxis(da, 2, -1))
    cb = jnp.einsum('bclgn,bcsgn->bcgls', cm, bm)
    y_diag = jnp.einsum('bcgls,bcgrls,bcsgrp->bclgrp', cb, decay, xdt)
    decay_to_end = jnp.exp(a_cs[:, :, -1:] - a_cs)
    states = jnp.einsum('bclgn,bclgr,bclgrp->bcgrpn', bm, decay_to_end, xdt)
    chunk_decay = jnp.exp(a_cs[:, :, -1])

    def step(h, inp):
        st, dec = inp
        return h * dec[..., None, None] + st, h

    h0 = jnp.zeros((bsz, g_, r_, p_, n_), jnp.float32)
    _, prev = lax.scan(step, h0, (jnp.moveaxis(states, 1, 0), jnp.moveaxis(chunk_decay, 1, 0)))
    prev = jnp.moveaxis(prev, 0, 1)
    y_off = jnp.einsum('bclgn,bcgrpn,bclgr->bclgrp', cm, prev, jnp.exp(a_cs))
    y = y_diag + y_off + d_skip.astype(jnp.float32).reshape(g_, r_)[:, :, None] * xs
    y = y.reshape(bsz, seq, SSD_D_INNER) * jax.nn.silu(z.astype(jnp.float32))
    y = rms_norm(y.reshape(bsz, seq, g_, SSD_D_INNER // g_), norm_w.reshape(g_, SSD_D_INNER // g_))
    y = y.reshape(bsz, seq, SSD_D_INNER).astype(u.dtype)
    return y @ w_out

def hgrn2_mixer(u, w_in, lb, norm_w, w_out):
    bsz, seq, _ = u.shape
    nc = seq // HGRN_CHUNK
    h_, k_dim, v_dim, c_ = HGRN_N_HEADS, HGRN_EXPAND, HGRN_HEAD_V, HGRN_CHUNK
    q, fz, v, g = jnp.split(u @ w_in, 4, axis=-1)
    fz = fz.astype(jnp.float32)
    lb = lb.astype(jnp.float32)
    log_f = jnp.logaddexp(jnp.log(lb), jnp.log1p(-lb) + jax.nn.log_sigmoid(fz))
    k = (1.0 - lb) * jax.nn.sigmoid(-fz)

    def chunked(t, d):
        return jnp.moveaxis(t.astype(jnp.float32).reshape(bsz, nc, c_, h_, d), 1, 0)

    qc, kc, vc = chunked(q, k_dim), chunked(k, k_dim), chunked(v, v_dim)
    b_cs = jnp.cumsum(chunked(log_f, k_dim), axis=2)
    mask = jnp.tril(jnp.ones((c_, c_), dtype=bool))[None, :, :, None, None]

    def step(s_prev, inp):
        q_, kk, v_, b_ = inp
        diff = b_[:, :, None] - b_[:, None, :]
        dec = jnp.exp(jnp.where(mask, diff, -jnp.inf))
        scores = jnp.einsum('blhk,bshk,blshk->bhls', q_, kk, dec)
        o = jnp.einsum('bhls,bshv->blhv', scores, v_) + jnp.einsum('blhk,bhkv->blhv', q_ * jnp.exp(b_), s_prev)
        b_last = b_[:, -1]
        s_new = jnp.exp(b_last)[..., None] * s_prev + jnp.einsum(
            'bshk,bshv->bhkv', kk * jnp.exp(b_last[:, None] - b_), v_)
        return s_new, o

    s0 = jnp.zeros((bsz, h_, k_dim, v_dim), jnp.float32)
    _, o = lax.scan(step, s0, (qc, kc, vc, b_cs))
    o = jnp.moveaxis(o, 0, 1).reshape(bsz, seq, h_, v_dim)
    o = rms_norm(o, norm_w).reshape(bsz, seq, D_MODEL) * jax.nn.silu(g.astype(jnp.float32))
    return o.astype(u.dtype) @ w_out

def sq_relu_mlp(h, w1, w2):
    a = jax.nn.relu(h @ w1)
    return (a * a) @ w2

def first_inputs(seed: int = 0) -> dict:
    key = jax.random.key(seed)
    ks = jax.random.split(key, 20)
    f32 = jnp.float32
    nrm = lambda k, shape, s: jax.random.normal(k, shape, f32) * s
    x = jax.random.normal(ks[0], (BATCH, SEQ, D_MODEL), f32)
    p = jax.random.normal(ks[1], (DEPTH, BATCH, SEQ, PLE_DIM), f32)
    ssd_w_in = nrm(ks[2], (N_SSD_LAYERS, D_MODEL, SSD_IN_DIM), D_MODEL ** -0.5)
    ssd_conv_w = nrm(ks[3], (N_SSD_LAYERS, SSD_CONV_WIDTH, SSD_CONV_DIM), SSD_CONV_WIDTH ** -0.5)
    ssd_conv_b = nrm(ks[4], (N_SSD_LAYERS, SSD_CONV_DIM), 0.02)
    dt0 = jnp.exp(jax.random.uniform(ks[5], (N_SSD_LAYERS, SSD_N_HEADS), f32,
                                     math.log(1e-3), math.log(1e-1)))
    ssd_dt_bias = dt0 + jnp.log(-jnp.expm1(-dt0))
    ssd_a_log = jnp.log(jax.random.uniform(ks[6], (N_SSD_LAYERS, SSD_N_HEADS), f32, 1.0, 16.0))
    ssd_d = 1.0 + nrm(ks[7], (N_SSD_LAYERS, SSD_N_HEADS), 0.02)
    ssd_norm_w = 1.0 + nrm(ks[8], (N_SSD_LAYERS, SSD_D_INNER), 0.02)
    ssd_w_out = nrm(ks[9], (N_SSD_LAYERS, SSD_D_INNER, D_MODEL), SSD_D_INNER ** -0.5 * DEEPNORM_BETA)
    hgrn_w_in = nrm(ks[10], (N_HGRN_LAYERS, D_MODEL, HGRN_IN_DIM), D_MODEL ** -0.5)
    hgrn_lower_bounds = nrm(ks[11], (N_HGRN_LAYERS, D_MODEL), 0.1)
    hgrn_norm_w = 1.0 + nrm(ks[12], (N_HGRN_LAYERS, HGRN_HEAD_V), 0.02)
    hgrn_w_out = nrm(ks[13], (N_HGRN_LAYERS, D_MODEL, D_MODEL), D_MODEL ** -0.5 * DEEPNORM_BETA)
    ln_g = 1.0 + nrm(ks[14], (DEPTH, 2, D_MODEL), 0.02)
    ln_b = nrm(ks[15], (DEPTH, 2, D_MODEL), 0.02)
    mlp_w1 = nrm(ks[16], (DEPTH, D_MODEL, D_FF), D_MODEL ** -0.5)
    mlp_w2 = nrm(ks[17], (DEPTH, D_FF, D_MODEL), D_FF ** -0.5 * DEEPNORM_BETA)
    ple_w_proj = nrm(ks[18], (DEPTH, PLE_DIM, D_MODEL), PLE_DIM ** -0.5)
    ple_w_gate = nrm(ks[19], (DEPTH, D_MODEL, D_MODEL), D_MODEL ** -0.5)
    return {"x": x, "p": p, "ssd_w_in": ssd_w_in, "ssd_conv_w": ssd_conv_w, "ssd_conv_b": ssd_conv_b,
            "ssd_dt_bias": ssd_dt_bias, "ssd_a_log": ssd_a_log, "ssd_d": ssd_d, "ssd_norm_w": ssd_norm_w,
            "ssd_w_out": ssd_w_out, "hgrn_w_in": hgrn_w_in, "hgrn_lower_bounds": hgrn_lower_bounds,
            "hgrn_norm_w": hgrn_norm_w, "hgrn_w_out": hgrn_w_out, "ln_g": ln_g, "ln_b": ln_b,
            "mlp_w1": mlp_w1, "mlp_w2": mlp_w2, "ple_w_proj": ple_w_proj, "ple_w_gate": ple_w_gate}

def first_block(x, p, ssd_w_in, ssd_conv_w, ssd_conv_b, ssd_dt_bias, ssd_a_log, ssd_d, ssd_norm_w,
              ssd_w_out, hgrn_w_in, hgrn_lower_bounds, hgrn_norm_w, hgrn_w_out, ln_g, ln_b,
              mlp_w1, mlp_w2, ple_w_proj, ple_w_gate):
    lbs = jnp.cumsum(jax.nn.softmax(hgrn_lower_bounds.astype(jnp.float32), axis=0), axis=0)
    lbs = lbs - lbs[0:1]
    for i in range(DEPTH):
        j = i // N_MIXERS
        if i % N_MIXERS == 0:
            mix = ssd_mixer(x, ssd_w_in[j], ssd_conv_w[j], ssd_conv_b[j], ssd_dt_bias[j], ssd_a_log[j],
                            ssd_d[j], ssd_norm_w[j], ssd_w_out[j])
        else:
            mix = hgrn2_mixer(x, hgrn_w_in[j], lbs[j], hgrn_norm_w[j], hgrn_w_out[j])
        h = layer_norm(DEEPNORM_ALPHA * x + mix, ln_g[i, 0], ln_b[i, 0])
        h = layer_norm(DEEPNORM_ALPHA * h + sq_relu_mlp(h, mlp_w1[i], mlp_w2[i]), ln_g[i, 1], ln_b[i, 1])
        x = h + jax.nn.sigmoid(h @ ple_w_gate[i]) * (p[i] @ ple_w_proj[i])
    return x


DEPTH_2 = 1

CHUNK = 64
N_META = 16
Q_BLOCK = 128
N_PAD = Q_BLOCK - N_META
PREFIX = N_PAD + N_META
MIX_WIDTH = D_MODEL
RET_HEADS = 4
RET_DV = (MIX_WIDTH // 2) // RET_HEADS
RET_DK = RET_DV // 2
FOX_HEADS = 8
FOX_DH = (MIX_WIDTH // 2) // FOX_HEADS
D_FF_2 = 2816
CONV_W = 3
ROPE_BASE = 10000.0
EPS = 1e-6
NEG = -1e30

RET_QK = RET_HEADS * RET_DK
RET_V = RET_HEADS * RET_DV
FOX_W = FOX_HEADS * FOX_DH
SPLIT_POINTS = (RET_QK, 2 * RET_QK, 2 * RET_QK + RET_V, 2 * RET_QK + 2 * RET_V,
                2 * RET_QK + 2 * RET_V + FOX_W, 2 * RET_QK + 2 * RET_V + 2 * FOX_W,
                2 * RET_QK + 2 * RET_V + 3 * FOX_W)
IN_WIDTH = 2 * RET_QK + 2 * RET_V + 3 * FOX_W + FOX_HEADS


def rms_norm_2(x, g):
    xf = x.astype(jnp.float32)
    y = xf * lax.rsqrt(jnp.mean(xf * xf, axis=-1, keepdims=True) + EPS)
    return (y * g.astype(jnp.float32)).astype(x.dtype)

def rotary(x, pos):
    half = x.shape[-1] // 2
    inv = 1.0 / (ROPE_BASE ** (jnp.arange(half, dtype=jnp.float32) / half))
    ang = pos.astype(jnp.float32)[:, None] * inv[None, :]
    cos = jnp.cos(ang)[None, :, None, :]
    sin = jnp.sin(ang)[None, :, None, :]
    x1 = x[..., :half].astype(jnp.float32)
    x2 = x[..., half:].astype(jnp.float32)
    return jnp.concatenate([x1 * cos - x2 * sin, x1 * sin + x2 * cos], axis=-1)

def retention(q, k, v, valid):
    B, L, H, dk = q.shape
    dv = v.shape[-1]
    nc = L // CHUNK
    f32 = jnp.float32
    log_g = jnp.log1p(-jnp.exp2(-5.0 - jnp.arange(H, dtype=f32)))
    pos = jnp.arange(L)
    qr = rotary(q, pos)
    kr = rotary(k, pos) * (dk ** -0.5) * valid.astype(f32)[None, :, None, None]
    qc = qr.reshape(B, nc, CHUNK, H, dk)
    kc = kr.reshape(B, nc, CHUNK, H, dk)
    vc = v.astype(f32).reshape(B, nc, CHUNK, H, dv)
    n = jnp.arange(CHUNK, dtype=f32)
    d_intra = jnp.exp(jnp.abs(n[:, None] - n[None, :])[None] * log_g[:, None, None])
    s = jnp.einsum('bcnhd,bcmhd->bchnm', qc, kc) * d_intra[None, None]
    intra = jnp.einsum('bchnm,bcmhe->bcnhe', s, vc)
    w_k = jnp.exp((CHUNK - 1.0 - n)[:, None] * log_g[None, :])
    u = jnp.einsum('bcmhd,bcmhe->bchde', kc * w_k[None, None, :, :, None], vc)
    g_chunk = jnp.exp(CHUNK * log_g)[None, :, None, None]

    def step(r, u_i):
        return g_chunk * r + u_i, r

    _, r_prev = lax.scan(step, jnp.zeros((B, H, dk, dv), f32), jnp.moveaxis(u, 1, 0))
    r_prev = jnp.moveaxis(r_prev, 0, 1)
    w_q = jnp.exp((n + 1.0)[:, None] * log_g[None, :])
    inter = jnp.einsum('bcnhd,bchde->bcnhe', qc * w_q[None, None, :, :, None], r_prev)
    return (intra + inter).reshape(B, L, H, dv)

def forgetting_attention(q, k, v, log_f, valid):
    B, L, H, dh = q.shape
    f32 = jnp.float32
    scale = dh ** -0.5
    c = jnp.cumsum(log_f.astype(f32), axis=1).transpose(0, 2, 1)
    qf, kf, vf = q.astype(f32), k.astype(f32), v.astype(f32)
    pos = jnp.arange(L)
    outs = []
    for blk in range(L // Q_BLOCK):
        q0, q1 = blk * Q_BLOCK, (blk + 1) * Q_BLOCK
        logits = jnp.einsum('bqhd,bkhd->bhqk', qf[:, q0:q1], kf[:, :q1]) * scale
        bias = c[:, :, q0:q1, None] - c[:, :, None, :q1]
        mask = (pos[None, :q1] <= pos[q0:q1, None]) & valid[None, :q1]
        logits = jnp.where(mask[None, None], logits + bias, NEG)
        p = jax.nn.softmax(logits, axis=-1)
        outs.append(jnp.einsum('bhqk,bkhd->bqhd', p, vf[:, :q1]))
    return jnp.concatenate(outs, axis=1)

def hybrid_mixer(h, w_in, forget_b, ret_norm_g, w_out, valid):
    B, L, _ = h.shape
    proj = jnp.einsum('bld,de->ble', h, w_in)
    rq, rk, rv, rg, fq, fk, fv, ff = jnp.split(proj, SPLIT_POINTS, axis=-1)
    o_r = retention(rq.reshape(B, L, RET_HEADS, RET_DK), rk.reshape(B, L, RET_HEADS, RET_DK),
                    rv.reshape(B, L, RET_HEADS, RET_DV), valid)
    o_r = o_r * lax.rsqrt(jnp.mean(o_r * o_r, axis=-1, keepdims=True) + EPS)
    o_r = o_r.reshape(B, L, RET_V) * ret_norm_g.astype(jnp.float32) * jax.nn.silu(rg.astype(jnp.float32))
    log_f = jax.nn.log_sigmoid(ff.astype(jnp.float32) + forget_b.astype(jnp.float32))
    o_f = forgetting_attention(fq.reshape(B, L, FOX_HEADS, FOX_DH), fk.reshape(B, L, FOX_HEADS, FOX_DH),
                               fv.reshape(B, L, FOX_HEADS, FOX_DH), log_f, valid).reshape(B, L, FOX_W)
    mixed = jnp.concatenate([o_r, o_f], axis=-1).astype(h.dtype)
    return jnp.einsum('ble,ed->bld', mixed, w_out)

def conv_ffn(h, w_up, conv_w, conv_b, w_down, valid):
    L = h.shape[1]
    up = jnp.einsum('bld,df->blf', h, w_up)
    a, b = jnp.split(up, 2, axis=-1)
    a = a * valid.astype(a.dtype)[None, :, None]
    a_pad = jnp.pad(a, ((0, 0), (CONV_W - 1, 0), (0, 0)))
    acc = conv_b
    for j in range(CONV_W):
        acc = acc + a_pad[:, j:j + L] * conv_w[j]
    return jnp.einsum('blf,fd->bld', jax.nn.silu(acc) * b, w_down)

def second_inputs(seed: int = 0) -> dict:
    key = jax.random.key(seed)
    ks = jax.random.split(key, 13)
    f32 = jnp.float32
    return {
        "x": jax.random.normal(ks[0], (BATCH, SEQ, D_MODEL), f32),
        "meta_tokens": jax.random.normal(ks[1], (N_META, D_MODEL), f32),
        "attn_norm_g": 1.0 + 0.02 * jax.random.normal(ks[2], (DEPTH_2, D_MODEL), f32),
        "w_in": jax.random.normal(ks[3], (DEPTH_2, D_MODEL, IN_WIDTH), f32) * D_MODEL ** -0.5,
        "fox_forget_b": jax.random.uniform(ks[4], (DEPTH_2, FOX_HEADS), f32, 1.0, 5.0),
        "ret_norm_g": 1.0 + 0.02 * jax.random.normal(ks[5], (DEPTH_2, RET_V), f32),
        "w_out": jax.random.normal(ks[6], (DEPTH_2, MIX_WIDTH, D_MODEL), f32) * MIX_WIDTH ** -0.5,
        "ffn_norm_g": 1.0 + 0.02 * jax.random.normal(ks[7], (DEPTH_2, D_MODEL), f32),
        "w_up": jax.random.normal(ks[8], (DEPTH_2, D_MODEL, 2 * D_FF_2), f32) * D_MODEL ** -0.5,
        "conv_w": jax.random.normal(ks[9], (DEPTH_2, CONV_W, D_FF_2), f32) * CONV_W ** -0.5,
        "conv_b": 0.02 * jax.random.normal(ks[10], (DEPTH_2, D_FF_2), f32),
        "w_down": jax.random.normal(ks[11], (DEPTH_2, D_FF_2, D_MODEL), f32) * D_FF_2 ** -0.5,
        "final_norm_g": 1.0 + 0.02 * jax.random.normal(ks[12], (D_MODEL,), f32),
    }

def second_block(x, meta_tokens, attn_norm_g, w_in, fox_forget_b, ret_norm_g, w_out,
              ffn_norm_g, w_up, conv_w, conv_b, w_down, final_norm_g):
    B = x.shape[0]
    pad = jnp.zeros((B, N_PAD, D_MODEL), x.dtype)
    meta = jnp.broadcast_to(meta_tokens.astype(x.dtype)[None], (B, N_META, D_MODEL))
    h = jnp.concatenate([pad, meta, x], axis=1)
    valid = jnp.arange(h.shape[1]) >= N_PAD
    for layer in range(DEPTH_2):
        h = h + hybrid_mixer(rms_norm_2(h, attn_norm_g[layer]), w_in[layer], fox_forget_b[layer],
                             ret_norm_g[layer], w_out[layer], valid)
        h = h + conv_ffn(rms_norm_2(h, ffn_norm_g[layer]), w_up[layer], conv_w[layer], conv_b[layer],
                         w_down[layer], valid)
    return rms_norm_2(h, final_norm_g)[:, PREFIX:]


def setup_inputs(seed=0):
    out = dict(first_inputs(seed))
    for name, value in second_inputs(seed + 1).items():
        if name != "x":
            out[name + "_2"] = value
    return out


def reference(
    x, p, ssd_w_in, ssd_conv_w, ssd_conv_b, ssd_dt_bias, ssd_a_log, ssd_d, ssd_norm_w,
    ssd_w_out, hgrn_w_in, hgrn_lower_bounds, hgrn_norm_w, hgrn_w_out, ln_g, ln_b, mlp_w1,
    mlp_w2, ple_w_proj, ple_w_gate, meta_tokens_2, attn_norm_g_2, w_in_2, fox_forget_b_2,
    ret_norm_g_2, w_out_2, ffn_norm_g_2, w_up_2, conv_w_2, conv_b_2, w_down_2, final_norm_g_2,
):
    x = first_block(
        x, p, ssd_w_in, ssd_conv_w, ssd_conv_b, ssd_dt_bias, ssd_a_log, ssd_d, ssd_norm_w,
        ssd_w_out, hgrn_w_in, hgrn_lower_bounds, hgrn_norm_w, hgrn_w_out, ln_g, ln_b, mlp_w1,
        mlp_w2, ple_w_proj, ple_w_gate,
    )
    return second_block(
        x, meta_tokens_2, attn_norm_g_2, w_in_2, fox_forget_b_2, ret_norm_g_2, w_out_2,
        ffn_norm_g_2, w_up_2, conv_w_2, conv_b_2, w_down_2, final_norm_g_2,
    )


_drawn_inputs = setup_inputs


def setup_inputs(seed=0):
    import zlib

    import numpy as np

    out = dict(_drawn_inputs(seed))
    spreads = {}
    factors = {'ssd_conv_b': 4.973,
     'ssd_d': 8.0,
     'ssd_norm_w': 7.175,
     'hgrn_norm_w': 8.0,
     'attn_norm_g_2': 3.463,
     'ret_norm_g_2': 7.634,
     'ffn_norm_g_2': 11.973,
     'conv_b_2': 33.252,
     'final_norm_g_2': 22.717}
    for name, (base, spread) in spreads.items():
        noise = np.random.default_rng([zlib.crc32(name.encode()), seed]).standard_normal(out[name].shape)
        drawn = base * np.exp(spread * noise) if base else spread * noise
        out[name] = __import__('jax').numpy.asarray(drawn.astype(out[name].dtype))
    for name, factor in factors.items():
        out[name] = (out[name] * factor).astype(out[name].dtype)
    return out
```

```python
from contextlib import ExitStack, contextmanager

import concourse.bass as bass
import numpy as np
from concourse import mybir
from concourse.alu_op_type import AluOpType as ALU

F32 = mybir.dt.float32
F32R = mybir.dt.float32r
U32 = mybir.dt.uint32
ACT = mybir.ActivationFunctionType
AX = mybir.AxisListType

P = 128
D = 1024
KD = D // P
T = 512
NCH = T // P
DEPTH = 2
ALPHA = float((2.0 * DEPTH) ** 0.25)
LN_EPS = 1e-5
EPS_2 = 1e-6
META = 16
L2 = META + T
H2 = L2 // 2
PAD = 112
DI = 2048
HEADS = 32
GROUPS = 4
HPG = HEADS // GROUPS
BLOCKS = 4
FF2 = 2816
F2T = FF2 // P
LEVELS = (64, 32, 16, 8, 4, 2, 1)
PROWS = (120, 109, 88)
N_PAR = 16
BASE = 1
FA_FFN = BASE + 4 * GROUPS + 2 * (BLOCKS * 8 + 8) + 8 + 2 * 8
FD_HGRN = BASE + GROUPS * 14 + BLOCKS * 8 + 8
FD_PROJ = FD_HGRN + 8 + 8 + BLOCKS * 8 + 8 + 24
FD_FFN = FD_PROJ + KD
FD_END = FD_FFN + F2T + 3 * KD
CA_IDENT, CA_TRI, CA_ONES, CA_MASK = 0, P, 2 * P, 3 * P
CA_W = (3 + len(LEVELS)) * P
CB_NEG, CB_ROT, CB_GAM = 0, P, 2 * P
CB_COS = CB_GAM + 4 * L2
CB_SIN = CB_COS + L2
CB_SEL = CB_SIN + L2
CB_W = CB_SEL + 8 * P


class Count:

    def __init__(self, base=0):
        self.n, self.per, self.iv, self.base = 0, 0, None, base

    def __call__(self, more=0):
        v = self.n + more + self.base
        return v if self.iv is None else self.iv * self.per + v

    def add(self, k=1):
        self.n += k


@contextmanager
def turns(eng, n, counts):
    with eng.Fori(0, n) as iv:
        start = {c: c.n for c in counts}
        for c, per in counts.items():
            c.iv, c.per = iv, per
        yield iv
        for c, per in counts.items():
            assert c.n == start[c] + per, (c.n - start[c], per)
            c.iv = None
    for c, per in counts.items():
        c.n = start[c] + n * per


class Own:

    def __init__(self, eng, sem):
        self.eng, self.sem, self.at = eng, sem, Count()

    def did(self, ins):
        ins.then_inc(self.sem, 1)
        self.at.add()

    def wait(self, back=0):
        self.eng.wait_ge(self.sem, self.at(-back))


def consts_a():
    i = np.arange(P)
    tri = (i[:, None] <= i[None, :])
    parts = [np.eye(P), tri, np.ones((P, P))]
    for m in LEVELS:
        same = (i[:, None] // (2 * m)) == (i[None, :] // (2 * m))
        parts.append(same & ((i[:, None] // m) % 2 == 0) & ((i[None, :] // m) % 2 == 1))
    return np.concatenate([q.astype(np.float32) for q in parts], 1)


def consts_b():
    i = np.arange(P)
    neg = np.where(i[None, :] > i[:, None], np.float32(-1e30), np.float32(0))
    rot = np.zeros((P, P), np.float32)
    for m in range(P):
        if m % 64 < 32:
            rot[m + 32, m] = -1.0
        else:
            rot[m - 32, m] = 1.0
    parts = [neg, rot]
    u = np.arange(L2)
    seen = ~((u[None, :] < 64) & (i[:, None] >= 64))
    for h in range(4):
        lg = np.log1p(-np.exp2(-5.0 - h))
        g = np.exp(np.abs(u[None, :] - i[:, None]) * lg) * (64 ** -0.5)
        parts.append(np.where(seen, g, 0.0))
    half = 32
    inv = (1.0 / (np.float32(10000.0) ** (np.arange(half, dtype=np.float32) / half))).astype(np.float32)
    ang = (np.arange(PAD, PAD + L2).astype(np.float32)[None, :] * inv[i % half][:, None]).astype(np.float32)
    parts += [np.cos(ang), np.sin(ang)]
    sel = np.zeros((P, 8, P), np.float32)
    for h in range(8):
        sel[h, h, :] = -1.0
    parts.append(sel.reshape(P, 8 * P))
    return np.concatenate([q.astype(np.float32) for q in parts], 1)


def two_blocks(nc, x, p, ssd_w_in, ssd_conv_w, ssd_conv_b, ssd_dt_bias, ssd_a_log, ssd_d, ssd_norm_w,
               ssd_w_out, hgrn_w_in, hgrn_norm_w, hgrn_w_out, ln_g, ln_b, mlp_w1, mlp_w2,
               ple_w_proj, ple_w_gate, meta_tokens, attn_norm_g, w_in_2, forget_b, ret_norm_g,
               w_out_2, ffn_norm_g, w_up, conv_w_2, conv_b_2, w_down, final_norm_g,
               const_a, const_b, out):
    ctx = ExitStack()
    with ctx:
        def sb(name, shape, dt=F32, where=ctx):
            return where.enter_context(nc.sbuf_tensor(name, shape, dt))

        def sem(name):
            return ctx.enter_context(nc.semaphore(name))

        raw = sb("raw", [P, 2, 2048])
        w_hi = sb("w_hi", [P, 2, 2048], F32R)
        w_lo = sb("w_lo", [P, 2, 2048], F32R)
        res = sb("res", [P, KD, L2])
        ident_tri = sb("consts", [P, CA_MASK])
        pcol = sb("pcol", [P, 3, P])
        ident = ident_tri[:, CA_IDENT:CA_IDENT + P]
        tri = ident_tri[:, CA_TRI:CA_TRI + P]
        ones = ident_tri[:, CA_ONES:CA_ONES + P]
        b_hi = sb("b_hi", [P, KD, L2], F32R)
        b_lo = sb("b_lo", [P, KD, L2], F32R)
        wff = sb("wff", [P, KD, 8])
        fb = sb("fb", [8, 1])
        lneps = sb("lneps", [P, 6])
        small = sb("small", [P, 512])

        def conv_col(w, t):
            return pcol[:, 0, w * 24 + t:w * 24 + t + 1]

        def col1(base, k):
            return pcol[:, 1, base + k:base + k + 1]
        C_NW, C_LG, C_LB, C_HN, C_AN, C_FN, C_FIN, C_RN = 0, 16, 48, 80, 81, 89, 97, 105

        dtp = small[:, 0:128].rearrange("p (c h) -> p c h", c=NCH)
        dap = small[:, 128:256].rearrange("p (c h) -> p c h", c=NCH)
        csp = sb("csp", [P, NCH, HEADS])
        dtep = sb("dtep", [P, NCH, HEADS])
        cdp = sb("cdp", [P, NCH, HEADS])
        bias32 = small[:, 256:288]
        nega = small[:, 288:320]
        dcol = small[:, 320:336]
        gx = small[:, 336:356].rearrange("p (w j) -> p w j", w=5)
        gb = small[:, 356:361]
        gc = small[:, 361:366]
        gn = small[:, 366:370]
        gd = small[:, 370:374]
        gdt = small[:, 376:408].rearrange("p (c h) -> p c h", c=NCH)
        gda = small[:, 408:440].rearrange("p (c h) -> p c h", c=NCH)
        gcs = small[:, 440:472].rearrange("p (c h) -> p c h", c=NCH)
        gdte = small[:, 472:504].rearrange("p (c h) -> p c h", c=NCH)
        d32 = sb("d32", [P, HEADS])
        gcd = sb("gcd", [P, NCH, HPG])
        cst = sb("cst", [HPG, T])
        sp0 = sb("sp0", [P, P])
        sp1 = sb("sp1", [P, P])
        bl4 = sb("bl4", [P, NCH])

        one = ExitStack()
        a_hi = sb("a_hi", [P, KD, L2], F32R, one)
        a_lo = sb("a_lo", [P, KD, L2], F32R, one)
        xc = sb("xc", [P, KD, L2], F32, one)
        ssd = ExitStack()
        zt = sb("zt", [P, 4, T], F32, ssd)
        xs = sb("xs", [P, 4, T], F32, ssd)
        bt = sb("bt", [P, T], F32, ssd)
        ct = sb("ct", [P, T], F32, ssd)
        xdt = sb("xdt", [P, NCH, T], F32, ssd)
        xdtd = sb("xdtd", [P, 2, T], F32, ssd)
        btok = sb("btok", [P, NCH, P], F32, ssd)
        hst = xc[:, 3:6, 0:T]
        cbm = sb("cbm", [P, NCH, P], F32, ssd)
        eh2 = sb("eh2", [P, 2, T], F32, ssd)
        eh = (eh2[:, 0], eh2[:, 1], xc[:, 0, 0:T])
        em = (xc[:, 6, 0:T], xc[:, 7, 0:T], xc[:, 1, 0:T])
        ssd.close()
        start = ExitStack()
        xtok = sb("xtok", [P, NCH, D], F32, start)
        wdt = sb("wdt", [P, KD, HEADS], F32, start)
        prow = sb("prow", [P, 3, P], F32, start)
        start.close()
        mlp = ExitStack()
        sq = sb("sq", [P, 4, L2], F32, mlp)
        lv = sb("lv", [P, L2], F32, mlp)
        hid = ExitStack()
        hu = sb("hu", [P, 2, T], F32, hid)
        hv = sb("hv", [P, 4, T], F32, hid)
        ptok = sb("ptok", [P, NCH, 256], F32, hid)
        pf = sb("pf", [P, 2, T], F32, hid)
        mtok = sb("mtok", [META, D], F32, hid)
        au = sb("au", [P, 516], F32, hid)
        acc = sb("acc", [P, T], F32, hid)
        otok = hv[:].rearrange("p (a b) n -> p a (b n)", a=2)
        hid.close()
        hg = ExitStack()
        hq = sb("hq", [P, T], F32, hg)
        hk = sb("hk", [P, T], F32, hg)
        hb = sb("hb", [P, T], F32, hg)
        hlf = sb("hlf", [P, T], F32, hg)
        hlk = sb("hlk", [P, T], F32, hg)
        hvf = sb("hvf", [P, T], F32, hg)
        hvt = sb("hvt", [P, NCH, P], F32, hg)
        hqe = sb("hqe", [P, T], F32, hg)
        hkd = sb("hkd", [P, T], F32, hg)
        hkt = sb("hkt", [P, NCH, P], F32, hg)
        hdd = sb("hdd", [P, 4, T], F32, hg)
        hsc = sb("hsc", [P, NCH, P], F32, hg)
        hst2 = sb("hst2", [P, 3, P], F32, hg)
        ho = sb("ho", [P, T], F32, hg)
        level_masks = sb("level_masks", [P, len(LEVELS) * P], F32, hg)
        masks = [level_masks[:, i * P:(i + 1) * P] for i in range(len(LEVELS))] + [ident]
        hg.close()
        mlp.close()
        pj = ExitStack()
        proj = sb("proj", [P, 24, L2], F32, pj)
        pj.close()
        one.close()

        mix = ExitStack()
        cb = sb("cb", [P, CB_SEL], F32, mix)
        sel = sb("sel", [8, 8 * P], F32, mix)
        negm = cb[:, CB_NEG:CB_NEG + P]
        rotm = cb[:, CB_ROT:CB_ROT + P]
        gam = cb[:, CB_GAM:CB_GAM + 4 * L2]
        cosr, sinr = cb[:, CB_COS:CB_COS + L2], cb[:, CB_SIN:CB_SIN + L2]
        fz = sb("fz", [8, L2], F32, mix)
        fl = sb("fl", [8, L2], F32, mix)
        fcs = sb("fcs", [8, L2], F32, mix)
        ret = ExitStack()
        rq, rk, rv0, rv1, ro, rsq = (sb(x, [P, L2], F32, ret) for x in ("rq", "rk", "rv0", "rv1", "ro", "rsq"))
        rsn = (rsq, ro)
        rvt = sb("rvt", [P, 5, 2 * P], F32, ret)
        rsm = [sb(f"rsm{i}", [P, L2 - (META + (i - 1) * P if i else 0)], F32, ret) for i in range(5)]
        ret.close()
        fox = ExitStack()
        fq, fk, fv, fo = (sb(x, [P, L2], F32, fox) for x in ("fq", "fk", "fv", "fo"))
        sel2 = sb("sel2", [8, 2 * P], F32, fox)
        fvt = sb("fvt", [P, 5, P], F32, fox)
        fp = sb("fp", [P, 2, L2], F32, fox)
        fpt = sb("fpt", [P, T], F32, fox)
        fpt0 = sb("fpt0", [META, P], F32, fox)
        fm = sb("fm", [P, 2, 4], F32, fox)
        fox.close()
        mix.close()

        ps = ctx.enter_context(nc.psum_tensor("ps", [P, 8, 512], F32))
        bank = [ps[:, i, :] for i in range(8)]

        cs_bank = (bank[4], bank[5], bank[3])
        s_mask, s_par, s_x, s_wdt, s_ptok = sem("masks_in"), sem("params_in"), sem("x_in"), sem("wdt_in"), sem("p_in")
        raw_in = [sem("raw_in0"), sem("raw_in1")]
        whi_ready, wlo_ready = sem("whi_ready"), sem("wlo_ready")
        tile_done = sem("tile_done")
        free_act, free_dve = sem("free_act"), sem("free_dve")
        xc_ready, ahi_ready, alo_ready, res_ready = (sem("xc_ready"), sem("ahi_ready"),
                                                     sem("alo_ready"), sem("res_ready"))
        bhi_ready, blo_ready = sem("bhi_ready"), sem("blo_ready")
        act_own, dve_own = sem("act_own"), sem("dve_own")
        mean_done, ln_xc, ln_sq, sq_used, rstd_ready = (sem("mean_done"), sem("ln_xc"), sem("ln_sq"),
                                                        sem("sq_used"), sem("rstd_ready"))
        pcol_done, pcol_ready = sem("pcol_done"), sem("pcol_ready")
        xt_done, dt_mm, da_ready, cs_mm, tot_mm, dt_tail = (sem("x_turned"), sem("dt_mm"), sem("da_ready"),
                                                            sem("cs_mm"), sem("tot_mm"), sem("dt_tail"))
        group_ready, hs_decayed, xs_ready = sem("group_ready"), sem("hs_decayed"), sem("xs_ready")
        xtok_done, xdt_ready, bt_done, bt_ready = (sem("xtok_done"), sem("xdt_ready"), sem("bt_done"),
                                                   sem("bt_ready"))
        cb_done, cbm_ready, cst_done, cst_ready = (sem("cb_done"), sem("cbm_ready"), sem("cst_done"),
                                                   sem("cst_ready"))
        xdtd_ready, st_done, hs_ready = sem("xdtd_ready"), sem("st_done"), sem("hs_ready")
        csbc_done, dm_ready, eh_ready, em_ready = (sem("csbc_done"), sem("dm_ready"), sem("eh_ready"),
                                                   sem("em_ready"))
        ch_ready, m_ready, y_mm, yv_ready, y_ready = (sem("ch_ready"), sem("m_ready"), sem("y_mm"),
                                                      sem("yv_ready"), sem("y_ready"))
        ysq_ready, yvar_done, yrstd_ready, yn_ready = (sem("ysq_ready"), sem("yvar_done"),
                                                       sem("yrstd_ready"), sem("yn_ready"))
        pt_done, pf_ready = sem("p_turned"), sem("pf_ready")

        l_ready, lf_ready, k_ready, b_ready = sem("l_ready"), sem("lf_ready"), sem("k_ready"), sem("b_ready")
        vt_done, vt_ready, qe_ready, kd_ready = sem("vt_done"), sem("vt_ready"), sem("qe_ready"), sem("kd_ready")
        eb_ready, ekd_ready, kt_done, kt_ready = sem("eb_ready"), sem("ekd_ready"), sem("kt_done"), sem("kt_ready")
        s_done, s_ready, s_step = sem("s_done"), sem("s_ready"), sem("s_step")
        dd_ready, ed_ready, w_ready, sc_done, sc_read = (sem("dd_ready"), sem("ed_ready"), sem("w_ready"),
                                                         sem("sc_done"), sem("sc_read"))
        o_done, osq_ready, ovar_done, orstd_ready, on_ready = (sem("o_done"), sem("osq_ready"), sem("ovar_done"),
                                                               sem("orstd_ready"), sem("on_ready"))
        NL = len(LEVELS)
        NS = NL + 1

        def halves_of(t, m, upper):
            return t.rearrange("p (n two m) -> p two n m", two=2, m=m)[:, 1 if upper else 0]

        def hgrn_pool(pool, chunk, b_at, cut_lo):
            for j in range(4):
                cut_lo((j + 1) % 2)
            cut_lo(1, 1024)
            cut_lo(0)

            def head(h, final):
                for i, m in enumerate(LEVELS):
                    pool.wait_ge(ed_ready, h * NL + (i + 1))
                    if i == 0:
                        pool.wait_ge(k_ready, h + 1)
                    d = hdd[:, i % 4]
                    nc.gpsimd.tensor_tensor(halves_of(d, m, True), halves_of(d, m, True),
                                            halves_of(hq[:], m, True), ALU.mult).then_inc(w_ready, 1)
                    nc.gpsimd.tensor_tensor(halves_of(d, m, False), halves_of(d, m, False),
                                            halves_of(hk[:], m, False), ALU.mult).then_inc(w_ready, 1)
                    if i == 1:
                        pool.wait_ge(ekd_ready, h + 1)
                        nc.gpsimd.tensor_tensor(hkd[:, 0:3 * P], hkd[:, 0:3 * P], hk[:, 0:3 * P],
                                                ALU.mult).then_inc(kd_ready, 1)
                    if i == 2:
                        nc.gpsimd.tensor_tensor(hqe[:, P:T], hqe[:, P:T], hq[:, P:T], ALU.mult).then_inc(qe_ready, 1)
                if not final:
                    cut_lo(1, 1024)
                    cut_lo(0)
                pool.wait_ge(bhi_ready, b_at(1))
                nc.gpsimd.tensor_tensor(b_lo[:, bass.ds(h, 1), 0:T], ho[:].unsqueeze(1),
                                        b_hi[:, bass.ds(h, 1), 0:T].bitcast(F32), ALU.subtract).then_inc(blo_ready, 1)
                b_at.add()

            with turns(pool, 7, {chunk: 2, b_at: 1}) as h:
                head(h, False)
            head(7, True)
            for j in range(4):
                cut_lo((j + 1) % 2)

        def hgrn_act(act, chunk, tile, fa, own, b_at, cut_hi):
            for j in range(4):
                cut_hi((j + 1) % 2)
                for m in range(2):
                    act.wait_ge(tile_done, tile(1))
                    nc.scalar.activation(xc[:, 2 * j + m, 0:T], bank[tile.n % 4], ACT.Silu).then_inc(free_act, 1)
                    fa.add()
                    tile.add()
            act.preload_act_table_set("natural_log_exp_and_others")
            cut_hi(1, 1024)
            tile.add(2)

            def forget():
                act.wait_ge(tile_done, tile())
                own.did(nc.scalar.activation(hlk[:], bank[1], ACT.Abs))
                own.wait()
                own.did(nc.scalar.activation(hlk[:], hlk[:], ACT.Exp, scale=-1.0))
                own.wait()
                nc.scalar.activation(hlk[:], hlk[:], ACT.Ln, bias=1.0).then_inc(l_ready, 1)
                cut_hi(0)

            def head(h, final):
                act.wait_ge(tile_done, tile())
                nc.scalar.activation(hq[:], bank[0], ACT.Copy).then_inc(free_act, 1)
                fa.add()
                act.wait_ge(tile_done, tile(1))
                nc.scalar.activation(hvf[:], bank[2], ACT.Copy).then_inc(free_act, 1)
                fa.add()
                tile.add()
                act.wait_ge(free_dve, h + (FD_HGRN + 1))
                nc.scalar.activation(hk[:], hlk[:], ACT.Exp, scale=-1.0).then_inc(k_ready, 1)

                def level(i):
                    act.wait_ge(dd_ready, h * (2 * NL) + (2 * i + 2))
                    nc.scalar.activation(hdd[:, i % 4], hdd[:, i % 4], ACT.Exp).then_inc(ed_ready, 1)

                level(0)
                level(1)
                for c in range(3):
                    last = nc.scalar.activation(hkd[:, c * P:(c + 1) * P], hb[:, c * P:(c + 1) * P], ACT.Exp,
                                                scale=-1.0, bias=hb[:, (c + 1) * P - 1:(c + 1) * P])
                last.then_inc(ekd_ready, 1)
                own.did(nc.scalar.activation(hqe[:, P:T], hb[:, P:T], ACT.Exp))
                nc.scalar.activation(bl4[:], hb[:].rearrange("p (c l) -> p c l", c=NCH)[:, :, P - 1], ACT.Exp
                                     ).then_inc(eb_ready, 1)
                level(2)
                level(3)
                if not final:
                    cut_hi(1, 1024)
                    tile.add(2)
                act.wait_ge(vt_done, h + 1)
                nc.scalar.activation(hvt[:], bank[4].rearrange("p (c v) -> p c v", c=NCH), ACT.Copy).then_inc(vt_ready, 1)
                act.wait_ge(kt_done, h + 1)
                nc.scalar.activation(hkt[:, 0:3], bank[5][:, 0:3 * P].rearrange("p (c k) -> p c k", c=3),
                                     ACT.Copy).then_inc(kt_ready, 1)
                for i in range(4, NL):
                    level(i)
                if not final:
                    forget()
                act.wait_ge(o_done, h + 1)
                own.did(nc.scalar.activation(ho[:], bank[6], ACT.Copy))
                own.wait()
                nc.scalar.activation(hkd[:], bank[6], ACT.Square).then_inc(osq_ready, 1)
                act.wait_ge(ovar_done, h + 1)
                own.did(nc.scalar.activation(hqe[:], bank[4], ACT.Ln, scale=1.0 / P, bias=lneps[:, 0:1]))
                own.wait()
                nc.scalar.activation(bank[5], hqe[:], ACT.Exp, scale=-0.5).then_inc(orstd_ready, 1)
                act.wait_ge(on_ready, h * 2 + 2)
                own.did(nc.scalar.activation(sp1[:, 0:1], ho[:, 0:1], ACT.Copy))
                nc.scalar.activation(b_hi[:, bass.ds(h, 1), 0:T], ho[:].unsqueeze(1), ACT.Copy).then_inc(bhi_ready, 1)
                b_at.add()

            forget()
            with turns(act, 7, {chunk: 2, tile: 3, fa: 2, own.at: 6, b_at: 1}) as h:
                head(h, False)
            head(7, True)
            for j in range(4):
                cut_hi((j + 1) % 2)
                tile.add(2)

        def hgrn_dve(dve, tile, fd, own, b_at, add_to_res):
            assert fd() == FD_HGRN
            tile.add(8)
            dve.wait_ge(s_mask, 16)

            def forget(n):
                f = bank[1]
                dve.wait_ge(l_ready, n + 1)
                nc.vector.scalar_tensor_tensor(out=hlf[:], in0=f, scalar=0.0, in1=hlk[:], op0=ALU.min,
                                               op1=ALU.subtract).then_inc(lf_ready, 1)
                nc.vector.scalar_tensor_tensor(out=hlk[:], in0=f, scalar=0.0, in1=hlk[:], op0=ALU.max,
                                               op1=ALU.add).then_inc(free_dve, 1)
                dve.wait_ge(lf_ready, n + 1)
                for c in range(NCH):
                    cols = slice(c * P, (c + 1) * P)
                    last = nc.vector.tensor_tensor_scan(hb[:, cols], ones, hlf[:, cols], 0.0, ALU.mult, ALU.add)
                last.then_inc(b_ready, 1)
                fd.add()

            def head(h, final):
                tile.add(3)
                dve.wait_ge(b_ready, h + 1)

                def level(i, before=None):
                    m = LEVELS[i]
                    if i >= 4:
                        dve.wait_ge(sc_done, h * NS + (i - 3))
                    up, low = halves_of(hb[:], m, True), halves_of(hb[:], m, False)
                    ref = low[:, :, m - 1:m].broadcast_to([P, T // (2 * m), m])
                    nc.vector.tensor_tensor(halves_of(hdd[:, i % 4], m, True), up, ref,
                                            ALU.subtract).then_inc(dd_ready, 1)
                    if before:
                        dve.wait_ge(*before)
                    nc.vector.tensor_tensor(halves_of(hdd[:, i % 4], m, False), ref, low,
                                            ALU.subtract).then_inc(dd_ready, 1)

                def scores(i):
                    src = bank[7 if i % 2 == 0 else 3].rearrange("p (c l) -> p c l", c=NCH)
                    mask = masks[i].unsqueeze(1).broadcast_to([P, NCH, P])
                    if i == 0:
                        nc.vector.tensor_tensor(hsc[:], src, mask, ALU.mult).then_inc(sc_read, 1)
                    else:
                        nc.vector.copy_predicated(hsc[:], mask.bitcast(U32), src).then_inc(sc_read, 1)

                for i in range(4):
                    level(i)
                for i in range(NS):
                    if i + 4 < NL:
                        level(i + 4, (sc_read, h * NS + i) if i else None)
                    else:
                        dve.wait_ge(sc_done, h * NS + (i + 1))
                        dve.wait_ge(sc_read, h * NS + i)
                        nc.vector.tensor_copy(sp0[:, i:i + 1], ones[:, 0:1])
                    scores(i)
                    if i == 2:
                        dve.wait_ge(s_done, h + 1)
                        dve.wait_ge(eb_ready, h + 1)
                        nc.vector.tensor_copy(hst2[:, 0], bank[6][:, 0:P]).then_inc(s_step, 1)
                        for c in (1, 2):
                            dve.wait_ge(s_step, h * 3 + c)
                            nc.vector.scalar_tensor_tensor(out=hst2[:, c], in0=hst2[:, c - 1], scalar=bl4[:, c:c + 1],
                                                           in1=bank[6][:, c * P:(c + 1) * P], op0=ALU.mult,
                                                           op1=ALU.add).then_inc(s_step, 1)
                if not final:
                    forget(h + 1)
                dve.wait_ge(orstd_ready, h + 1)
                nc.vector.scalar_tensor_tensor(out=ho[:], in0=ho[:], scalar=col1(C_HN, 0), in1=bank[5],
                                               op0=ALU.mult, op1=ALU.mult).then_inc(on_ready, 1)
                dve.wait_ge(on_ready, h * 2 + 1)
                nc.vector.tensor_tensor(ho[:].unsqueeze(1), ho[:].unsqueeze(1), xc[:, bass.ds(h, 1), 0:T],
                                        ALU.mult).then_inc(on_ready, 1)
                b_at.add()

            forget(0)
            with turns(dve, 7, {tile: 3, fd: 1, own.at: 0, b_at: 1}) as h:
                head(h, False)
            head(7, True)
            add_to_res(8)

        def hgrn_pe(pe, chunk, tile, fa, fd, pe_turns, b_at, chunk_mm):
            for j in range(4):
                chunk_mm(j % 2, KD, 256, (a_hi, a_lo), fa, ready=(alo_ready, 3 * KD) if j == 0 else None)
            def q_f():
                chunk_mm(0, KD, 256, (a_hi, a_lo), (fa, fd), far=(fa.n, fd.n), geo=((0, 0, T, 1), (1, 0, T, 1)))

            def head(h, final):
                chunk_mm(1, KD, P, (a_hi, a_lo), fa, far=(fa.n - 1, fd.n - 1), geo=((2, 0, T, 1),))
                pe.wait_ge(free_act, fa())
                for c in range(NCH):
                    last = nc.tensor.transpose(bank[4][:, c * P:(c + 1) * P], hvf[:, c * P:(c + 1) * P], ident)
                last.then_inc(vt_done, 1)

                def score(i):
                    if i < NL:
                        pe.wait_ge(w_ready, h * (2 * NL) + (2 * i + 2))
                    if i >= 2:
                        pe.wait_ge(sc_read, h * NS + (i - 1))
                    for c in range(NCH):
                        cols = slice(c * P, (c + 1) * P)
                        k, q = (hdd[:, i % 4, cols], hdd[:, i % 4, cols]) if i < NL else (hk[:, cols], hq[:, cols])
                        last = nc.tensor.matmul(bank[7 if i % 2 == 0 else 3][:, cols], k, q, start=True, stop=True)
                    last.then_inc(sc_done, 1)

                score(0)
                score(1)
                pe.wait_ge(kd_ready, h + 1)
                for c in range(3):
                    last = nc.tensor.transpose(bank[5][:, c * P:(c + 1) * P], hkd[:, c * P:(c + 1) * P], ident)
                last.then_inc(kt_done, 1)
                score(2)
                pe.wait_ge(kt_ready, h + 1)
                pe.wait_ge(vt_ready, h + 1)
                for c in range(3):
                    last = nc.tensor.matmul(bank[6][:, c * P:(c + 1) * P], hkt[:, c], hvt[:, c], start=True, stop=True)
                last.then_inc(s_done, 1)
                if not final:
                    q_f()
                for i in range(3, NS):
                    score(i)
                pe.wait_ge(s_step, h * 3 + 3)
                pe.wait_ge(qe_ready, h + 1)
                pe.wait_ge(sc_read, h * NS + NS)
                for c in range(NCH):
                    cols = slice(c * P, (c + 1) * P)
                    last = nc.tensor.matmul(bank[6][:, cols], hvt[:, c], hsc[:, c], start=True, stop=(c == 0))
                    if c:
                        last = nc.tensor.matmul(bank[6][:, cols], hst2[:, c - 1], hqe[:, cols], start=False, stop=True)
                last.then_inc(o_done, 1)
                pe.wait_ge(osq_ready, h + 1)
                nc.tensor.matmul(bank[4], ones, hkd[:], start=True, stop=True).then_inc(ovar_done, 1)
                b_at.add()

            q_f()
            with pe_turns(7, {chunk: 2, tile: 3, fa: 2, fd: 1, b_at: 1}) as h:
                head(h, False)
            head(7, True)
            mark = (fa.n, fd.n)
            for j in range(4):
                chunk_mm(j % 2, KD, 256, (b_hi, b_lo), fd, far=mark if j < 2 else None, ready=(blo_ready, b_at(-KD)) if j == 0 else None)

        s_meta, s_ff, s_constb, s_out = sem("meta_in"), sem("ff_in"), sem("const_b_in"), (sem("out_written0"), sem("out_written1"))
        meta_done, ff_done, ff_ready, fl_ready, ct_ready = (sem("meta_turned"), sem("ff_done"), sem("ff_ready"),
                                                            sem("fl_ready"), sem("ct_ready"))
        r_in, r_rot, r_cos, r_sin, r_rope = sem("r_in"), sem("r_rot"), sem("r_cos"), sem("r_sin"), sem("r_rope")
        r_vt, r_vtok, r_s, r_sm, r_o = sem("r_vt"), sem("r_vtok"), sem("r_s"), sem("r_sm"), sem("r_o")
        r_osq, r_var, r_rstd, r_on, r_gate = sem("r_osq"), sem("r_var"), sem("r_rstd"), sem("r_on"), sem("r_gate")
        f_in, f_vt, f_vtok, f_log, f_max, f_exp = (sem("f_in"), sem("f_vt"), sem("f_vtok"), sem("f_log"),
                                                   sem("f_max"), sem("f_exp"))
        f_pn, f_pt, f_pts, f_pts0, f_av, f_o = (sem("f_pn"), sem("f_pt"), sem("f_pts"), sem("f_pts0"),
                                                sem("f_av"), sem("f_o"))
        acc_ready, acc_act = sem("acc_ready"), sem("acc_act")
        ot_done, ot_ready = sem("ot_done"), sem("ot_ready")
        RES_ALL = 7 * KD + 1
        flat = ps[:, :, :].rearrange("p b n -> p (b n)")
        ROUNDS = ((8, 0), (8, 8), (6, 16))

        def two(t):
            return t.rearrange("p (s n) -> p s n", s=2)

        def pair(b, rows=P, n=H2):
            return ps[0:rows, b:b + 2, 0:n]

        def key_block(i):
            return (0, META) if i == 0 else (META + (i - 1) * P, P)

        def block2_sync(sp, chunk, load_cols, load_pair, kpn):
            w = kpn(w_in_2[0])
            with turns(sp, 6, {chunk: 2}) as i:
                for j in range(2):
                    load_cols(j, w, KD, i * 512 + j * 256, 256)
            for j in range(4):
                load_cols(j % 2, kpn(w_out_2[0]), KD, j * 256, 256)
            up, down = kpn(w_up[0]), kpn(w_down[0])

            def ffn(nt, t0):
                for j in range(nt):
                    load_pair(j % 2, up, t0 + j * P, t0 + (FF2 + j * P))
                for j in range(4):
                    load_cols(j % 2, down, nt, j * 256, 256, k0=k0)

            with turns(sp, 2, {chunk: 12}) as r:
                k0 = r * 8
                ffn(8, r * 1024)
            k0 = 16
            ffn(6, 2048)
            for c in range(NCH):
                sp.wait_ge(ot_ready, 2 * (c + 1))
                sp.dma_start(out[0, c * P:(c + 1) * P, :], otok[:, c % 2, :]).then_inc(s_out[c % 2], 16)
            for s in s_out:
                sp.wait_ge(s, 16 * NCH // 2)

        def block2_pool(pool, chunk, pub, b_at, cut_lo):
            def publish2_lo():
                for k in range(KD):
                    pool.wait_ge(ahi_ready, pub(1))
                    nc.gpsimd.tensor_tensor(a_lo[:, k, :], xc[:, k, :], a_hi[:, k, :].bitcast(F32),
                                            ALU.subtract).then_inc(alo_ready, 1)
                    pub.add()

            publish2_lo()
            with turns(pool, 6, {chunk: 2}):
                cut_lo(1)
                cut_lo(0)
            pool.wait_ge(s_constb, 32)
            with turns(pool, 2, {b_at: 2}) as i:
                for e, t in enumerate((rq, rk)):
                    pool.wait_ge(r_in, i * 4 + (e + 1))
                    pool.wait_ge(r_rot, i * 2 + (e + 1))
                    nc.gpsimd.tensor_tensor(t[:], t[:], cosr, ALU.mult).then_inc(r_cos, 1)
                for e in range(2):
                    pool.wait_ge(bhi_ready, b_at(1))
                    nc.gpsimd.tensor_tensor(b_lo[:, bass.ds(i * 2 + e, 1), :], ro[:].unsqueeze(1),
                                            b_hi[:, bass.ds(i * 2 + e, 1), :].bitcast(F32),
                                            ALU.subtract).then_inc(blo_ready, 1)
                    b_at.add()
            with turns(pool, 4, {b_at: 1}) as i:
                pool.wait_ge(bhi_ready, b_at(1))
                nc.gpsimd.tensor_tensor(b_lo[:, bass.ds(i + 4, 1), :], fo[:].unsqueeze(1),
                                        b_hi[:, bass.ds(i + 4, 1), :].bitcast(F32), ALU.subtract).then_inc(blo_ready, 1)
                b_at.add()
            for j in range(4):
                cut_lo((j + 1) % 2)
            publish2_lo()

            def ffn(nt, last):
                for j in range(nt):
                    cut_lo((j + 1) % 2, 2048 if j < nt - 1 else nt * 256)
                    pool.wait_ge(bhi_ready, b_at(1))
                    nc.gpsimd.tensor_tensor(b_lo[:, j, 0:T], hv[:, j % 4], b_hi[:, j, 0:T].bitcast(F32),
                                            ALU.subtract).then_inc(blo_ready, 1)
                    b_at.add()
                for j in range(4):
                    if j < 3 or not last:
                        cut_lo((j + 1) % 2, nt * 256 if j < 3 else 2048)

            with turns(pool, 2, {chunk: 12, b_at: 8}):
                ffn(8, False)
            ffn(6, True)

        def block2_act(act, chunk, tile, fa, own, pub, b_at, sq_at, cut_hi):
            def rms2_act(there, before):
                act.preload_act_table_set("natural_log_exp_and_others")
                for k in range(KD):
                    act.wait_ge(there, before + k + 1)
                    act.wait_ge(sq_used, sq_at(k - 3 if k >= 4 else 0))
                    nc.scalar.activation(sq[:, k % 4, :], res[:, k, :], ACT.Square).then_inc(ln_sq, 1)
                sq_at.add(KD)
                act.wait_ge(sq_used, sq_at())
                own.did(nc.scalar.activation(two(lv[:]), pair(4), ACT.Ln, scale=1.0 / D, bias=lneps[:, 1:2]))
                own.wait()
                nc.scalar.activation(pair(6), two(lv[:]), ACT.Exp, scale=-0.5).then_inc(rstd_ready, 1)

            def publish2():
                for k in range(KD):
                    act.wait_ge(xc_ready, pub(1))
                    nc.scalar.activation(a_hi[:, k, :], xc[:, k, :], ACT.Copy).then_inc(ahi_ready, 1)
                    pub.add()

            for k in range(KD):
                act.wait_ge(xc_ready, pub(1))
                nc.scalar.activation(res[:, k, META:], xc[:, k, 0:T], ACT.Copy).then_inc(res_ready, 1)
                pub.add()
            act.wait_ge(meta_done, 1)
            nc.scalar.activation(res[:, :, 0:META], bank[7][:, 0:P].rearrange("p (k n) -> p k n", k=KD),
                                 ACT.Copy).then_inc(res_ready, 1)
            act.wait_ge(res_ready, RES_ALL)
            rms2_act(res_ready, RES_ALL - KD)
            publish2()
            with turns(act, 6, {chunk: 2, tile: 4}):
                cut_hi(1)
                tile.add(2)
                cut_hi(0)
                tile.add(2)
            act.wait_ge(tile_done, tile())
            act.dma_start(cb[:], const_b[:, 0:CB_SEL]).then_inc(s_constb, 16)
            act.dma_start(sel[:], const_b[0:8, CB_SEL:CB_W]).then_inc(s_constb, 16)
            act.wait_ge(ff_done, 1)
            own.did(nc.scalar.activation(two(fz[:]), pair(4, 8), ACT.Identity, bias=fb[:]))
            own.wait()
            own.did(nc.scalar.activation(fl[:], fz[:], ACT.Abs))
            own.wait()
            own.did(nc.scalar.activation(fl[:], fl[:], ACT.Exp, scale=-1.0))
            own.wait()
            nc.scalar.activation(fl[:], fl[:], ACT.Ln, bias=1.0).then_inc(fl_ready, 1)
            act.wait_ge(free_dve, FD_PROJ)
            nc.scalar.activation(proj[:, 8:12], proj[:, 8:12], ACT.Silu).then_inc(r_gate, 1)
            act.preload_act_table_set("natural_log_exp_and_others")
            with turns(act, 2, {own.at: 7, b_at: 2}) as i:
                act.wait_ge(blo_ready, b_at())
                own.did(nc.scalar.activation(bl4[:], lneps[:, 0:1].broadcast_to([P, NCH]), ACT.Copy))
                for e, (dst, at) in enumerate(((rq, i), (rk, i + 2), (rv0, i * 2 + 4), (rv1, i * 2 + 5))):
                    nc.scalar.activation(dst[:].unsqueeze(1), proj[:, bass.ds(at, 1), :], ACT.Copy).then_inc(r_in, 1)
                act.wait_ge(r_vt, i * 2 + 2)
                for e in range(2):
                    nc.scalar.activation(rvt[:, 1:5, e * P:(e + 1) * P],
                                         bank[4 + e].rearrange("p (c v) -> p c v", c=NCH), ACT.Copy).then_inc(r_vtok, 1)
                nc.scalar.activation(rvt[0:META, 0, :], bank[6][0:META, 0:2 * P], ACT.Copy).then_inc(r_vtok, 1)
                for e in range(2):
                    act.wait_ge(r_o, i * 2 + (e + 1))
                    if e:
                        act.wait_ge(blo_ready, b_at())
                    own.did(nc.scalar.activation(two(ro[:]), pair(4 + 2 * e), ACT.Copy))
                    own.wait()
                    nc.scalar.activation(two(rsq[:]), pair(4 + 2 * e), ACT.Square).then_inc(r_osq, 1)
                    act.wait_ge(r_var, i * 2 + (e + 1))
                    own.did(nc.scalar.activation(two(rsq[:]), pair(0), ACT.Ln, scale=1.0 / P, bias=lneps[:, 1:2]))
                    own.wait()
                    nc.scalar.activation(pair(2), two(rsq[:]), ACT.Exp, scale=-0.5).then_inc(r_rstd, 1)
                    act.wait_ge(r_on, i * 4 + (2 * e + 2))
                    own.did(nc.scalar.activation(bl4[:, 0:1], ro[:, 0:1], ACT.Copy))
                    nc.scalar.activation(b_hi[:, bass.ds(i * 2 + e, 1), :], ro[:].unsqueeze(1),
                                         ACT.Copy).then_inc(bhi_ready, 1)
                    b_at.add()
            with turns(act, 4, {own.at: 4, b_at: 1}) as i:
                act.wait_ge(blo_ready, b_at())
                own.did(nc.scalar.activation(bl4[:], lneps[:, 0:1].broadcast_to([P, NCH]), ACT.Copy))
                nc.scalar.activation(fq[:].unsqueeze(1), proj[:, bass.ds(i + 12, 1), :], ACT.Copy,
                                     scale=64 ** -0.5).then_inc(f_in, 1)
                nc.scalar.activation(fk[:].unsqueeze(1), proj[:, bass.ds(i + 16, 1), :], ACT.Copy).then_inc(f_in, 1)
                nc.scalar.activation(fv[:].unsqueeze(1), proj[:, bass.ds(i + 20, 1), :], ACT.Copy).then_inc(f_in, 1)
                nc.scalar.activation(sel2[:], sel[:, bass.ds(i * 256, 256)], ACT.Copy).then_inc(f_in, 1)
                act.wait_ge(f_vt, i + 1)
                nc.scalar.activation(fvt[:, 1:5, :], bank[7].rearrange("p (c v) -> p c v", c=NCH),
                                     ACT.Copy).then_inc(f_vtok, 1)
                nc.scalar.activation(fvt[0:META, 0, :], bank[6][0:META, 0:P], ACT.Copy).then_inc(f_vtok, 1)

                def exps(n):
                    qb = n % 5
                    q, nk = key_block(qb)[1], META + P * qb
                    act.wait_ge(f_max, i * 10 + (n + 1))
                    if n >= 2:
                        act.wait_ge(f_pt, i * 10 + (n - 1))
                    nc.scalar.activation(fp[0:q, n % 2, 0:nk], flat[0:q, (n % 2) * 1024 + 112:(n % 2) * 1024 + 112 + nk],
                                         ACT.Exp, bias=fm[0:q, n % 2, 1:2],
                                         accum_out=fm[0:q, n % 2, 2:3]).then_inc(f_exp, 1)

                exps(0)
                exps(1)
                for n in range(10):
                    act.wait_ge(f_pt, i * 10 + (n + 1))
                    if n:
                        act.wait_ge(f_av, i * 10 + n)
                    q = key_block(n % 5)[1]
                    nc.scalar.activation(fpt0[:, 0:q], bank[5][0:META, 0:q], ACT.Copy).then_inc(f_pts0, 1)
                    if n + 2 < 10:
                        exps(n + 2)
                act.wait_ge(f_av, i * 10 + 10)
                own.did(nc.scalar.activation(fo[:, 0:META], bank[6][:, 0:META], ACT.Copy))
                own.did(nc.scalar.activation(fo[:, META:], bank[7], ACT.Copy))
                own.wait()
                own.did(nc.scalar.activation(bl4[:, 0:1], fo[:, 0:1], ACT.Copy))
                nc.scalar.activation(b_hi[:, bass.ds(i + 4, 1), :], fo[:].unsqueeze(1), ACT.Copy).then_inc(bhi_ready, 1)
                b_at.add()
            for j in range(4):
                cut_hi((j + 1) % 2)
                tile.add(2)
            rms2_act(free_dve, FD_PROJ)
            publish2()

            def ffn(nt, base, g0, last):
                for j in range(nt):
                    cut_hi((j + 1) % 2, 2048 if j < nt - 1 else nt * 256)
                    act.wait_ge(tile_done, tile(1))
                    act.wait_ge(free_dve, g0 + j)
                    b = 4 * (j % 2)
                    nc.scalar.activation(au[:].rearrange("p (s n) -> p s n", s=2), pair(b, P, 258),
                                         ACT.Copy).then_inc(free_act, 1)
                    fa.add()
                    act.wait_ge(acc_ready, base + (j + 1))
                    nc.scalar.activation(acc[:], acc[:], ACT.Silu).then_inc(acc_act, 1)
                    act.wait_ge(free_dve, g0 + (j + 1))
                    nc.scalar.activation(b_hi[:, j, 0:T], hv[:, j % 4], ACT.Copy).then_inc(bhi_ready, 1)
                    tile.add(2)
                    b_at.add()
                for j in range(4):
                    if j < 3 or not last:
                        cut_hi((j + 1) % 2, nt * 256 if j < 3 else 2048)
                    tile.add(2)

            with turns(act, 2, {chunk: 12, tile: 24, fa: 8, b_at: 8}) as r:
                ffn(8, r * 8, r * 16 + FD_FFN, False)
            ffn(6, 16, FD_FFN + 32, True)
            rms2_act(free_dve, FD_END - KD)
            for c in range(NCH):
                act.wait_ge(ot_done, 2 * c + 2)
                if c >= 2:
                    act.wait_ge(s_out[c % 2], 16)
                for s in range(2):
                    nc.scalar.activation(otok[:, c % 2, s * T:(s + 1) * T], bank[2 * (c % 2) + s],
                                         ACT.Copy).then_inc(ot_ready, 1)

        def block2_dve(dve, tile, fd, own, pub, b_at):
            def rms2_dve(i, col):
                dve.wait_ge(alo_ready, alo_all[i])
                dve.wait_ge(rstd_ready, 5 + i)
                for k in range(KD):
                    nc.vector.scalar_tensor_tensor(out=two(xc[:, k, :]), in0=two(res[:, k, :]), scalar=col1(col, k),
                                                   in1=pair(6), op0=ALU.mult, op1=ALU.mult).then_inc(xc_ready, 1)
                pub.add(KD)

            alo_all = (6 * KD, 7 * KD, 8 * KD)
            rms2_dve(0, C_AN)
            with turns(dve, 6, {tile: 4, fd: 4}) as i:
                for m in range(4):
                    dve.wait_ge(tile_done, tile(1))
                    nc.vector.tensor_scalar(proj[:, bass.ds(i * 4 + m, 1), :].rearrange("p a (s n) -> p (a s) n", s=2),
                                            pair(2 * (m % 2)), 1.0, None, ALU.mult).then_inc(free_dve, 1)
                    tile.add()
                    fd.add()
            assert fd() == FD_PROJ, fd()
            dve.wait_ge(fl_ready, 1)
            own.did(nc.vector.scalar_tensor_tensor(out=fz[:], in0=fz[:], scalar=0.0, in1=fl[:], op0=ALU.min,
                                                   op1=ALU.subtract))
            own.wait()
            own.did(nc.vector.memset(fl[:], 1.0))
            own.wait()
            nc.vector.tensor_tensor_scan(fcs[:], fl[:], fz[:], 0.0, ALU.mult, ALU.add).then_inc(ct_ready, 1)
            with turns(dve, 2, {own.at: 0, b_at: 2}) as i:
                for e, t in enumerate((rq, rk)):
                    dve.wait_ge(r_rot, i * 2 + (e + 1))
                    nc.vector.tensor_tensor(two(rsn[e][:]), pair(2 * e), two(sinr), ALU.mult).then_inc(r_sin, 1)
                for e, t in enumerate((rq, rk)):
                    dve.wait_ge(r_cos, i * 2 + (e + 1))
                    dve.wait_ge(r_sin, i * 2 + (e + 1))
                    nc.vector.tensor_tensor(t[:], t[:], rsn[e][:], ALU.add).then_inc(r_rope, 1)
                for e in range(2):
                    for kb in range(5):
                        k0, nk = key_block(kb)
                        n = L2 - k0
                        dve.wait_ge(r_s, i * 10 + (e * 5 + kb + 1))
                        if kb == 0:
                            if e:
                                dve.wait_ge(r_o, i * 2 + 1)
                            g = gam[0:META, bass.ds(i * (2 * L2) + e * L2, L2)]
                            ins = nc.vector.tensor_tensor(two(rsm[0][0:META, :]), pair(0, META), two(g), ALU.mult)
                        else:
                            g = gam[:, bass.ds(i * (2 * L2) + e * L2, n)]
                            ins = nc.vector.tensor_tensor(rsm[kb][:, 0:n], bank[2 + kb % 2][:, 0:n], g, ALU.mult)
                        ins.then_inc(r_sm, 1)
                    if e == 0:
                        dve.wait_ge(r_gate, 1)
                    dve.wait_ge(r_rstd, i * 2 + (e + 1))
                    nc.vector.scalar_tensor_tensor(out=two(ro[:]), in0=two(ro[:]),
                                                   scalar=pcol[:, 1, bass.ds(i * 2 + (C_RN + e), 1)], in1=pair(2),
                                                   op0=ALU.mult, op1=ALU.mult).then_inc(r_on, 1)
                    dve.wait_ge(r_on, i * 4 + (2 * e + 1))
                    nc.vector.tensor_tensor(ro[:].unsqueeze(1), ro[:].unsqueeze(1),
                                            proj[:, bass.ds(i * 2 + (8 + e), 1), :], ALU.mult).then_inc(r_on, 1)
                    b_at.add()
            with turns(dve, 4, {own.at: 20, b_at: 1}) as i:
                def maxes(n):
                    qb = n % 5
                    q, nk = key_block(qb)[1], META + P * qb
                    dve.wait_ge(f_log, i * 10 + (n + 1))
                    own.did(nc.vector.reduce_max(fm[0:q, n % 2, 0:1],
                                                 flat[0:q, (n % 2) * 1024 + 112:(n % 2) * 1024 + 112 + nk], AX.X))
                    own.wait()
                    nc.vector.tensor_scalar(fm[0:q, n % 2, 1:2], fm[0:q, n % 2, 0:1], -1.0, None,
                                            ALU.mult).then_inc(f_max, 1)

                def normed(n):
                    q, nk = key_block(n % 5)[1], META + P * (n % 5)
                    dve.wait_ge(f_exp, i * 10 + (n + 1))
                    own.did(nc.vector.reciprocal(fm[0:q, n % 2, 3:4], fm[0:q, n % 2, 2:3]))
                    own.wait()
                    nc.vector.tensor_scalar(fp[0:q, n % 2, 0:nk], fp[0:q, n % 2, 0:nk], fm[0:q, n % 2, 3:4], None,
                                            ALU.mult).then_inc(f_pn, 1)

                maxes(0)
                maxes(1)
                normed(0)
                for n in range(10):
                    qb = n % 5
                    if n + 1 < 10:
                        normed(n + 1)
                    if qb:
                        dve.wait_ge(f_pt, i * 10 + (n + 1))
                        if n:
                            dve.wait_ge(f_av, i * 10 + n)
                        nc.vector.tensor_copy(fpt[:, 0:qb * P], bank[4][:, 0:qb * P]).then_inc(f_pts, 1)
                    if n + 2 < 10:
                        maxes(n + 2)
                b_at.add()
            for m in range(KD):
                dve.wait_ge(tile_done, tile(1))
                nc.vector.tensor_tensor(two(res[:, m, :]), two(res[:, m, :]), pair(2 * (m % 2)),
                                        ALU.add).then_inc(free_dve, 1)
                tile.add()
                fd.add()
            rms2_dve(1, C_FN)

            def ffn(nt, base, t0):
                for j in range(nt):
                    taps = [pcol[:, 2, bass.ds(t0 + (w * F2T + j), 1)] for w in range(4)]
                    dve.wait_ge(free_act, FA_FFN + base + (j + 1))
                    dve.wait_ge(free_dve, fd())
                    own.did(nc.vector.tensor_scalar(acc[:], au[:, 4:516], taps[2], taps[3], ALU.mult, ALU.add))
                    own.wait()
                    own.did(nc.vector.scalar_tensor_tensor(out=acc[:], in0=au[:, 3:515], scalar=taps[1], in1=acc[:],
                                                           op0=ALU.mult, op1=ALU.add))
                    own.wait()
                    nc.vector.scalar_tensor_tensor(out=acc[:], in0=au[:, 2:514], scalar=taps[0], in1=acc[:],
                                                   op0=ALU.mult, op1=ALU.add).then_inc(acc_ready, 1)
                    tile.add()
                    dve.wait_ge(tile_done, tile(1))
                    dve.wait_ge(acc_act, base + (j + 1))
                    dve.wait_ge(blo_ready, b_at(-3))
                    nc.vector.tensor_tensor(hv[:, j % 4], acc[:], bank[2 + 4 * (j % 2)], ALU.mult).then_inc(free_dve, 1)
                    fd.add()
                    tile.add()
                    b_at.add()
                for m in range(8):
                    dve.wait_ge(tile_done, tile(1))
                    nc.vector.tensor_tensor(res[:, m, META:], res[:, m, META:], bank[tile.n % 4],
                                            ALU.add).then_inc(free_dve, 1)
                    tile.add()
                    fd.add()

            with turns(dve, 2, {tile: 24, fd: 16, own.at: 16, b_at: 8}) as r:
                ffn(8, r * 8, r * 8)
            ffn(6, 16, 16)
            assert fd() == FD_END, fd()
            rms2_dve(2, C_FIN)

        def block2_pe(pe, chunk, tile, fa, fd, pe_turns, b_at, chunk_mm, sq_at):
            def carry(b):
                nc.tensor.transpose(bank[b][:, 0:P], ident, ident)

            def rms2_pe():
                for k in range(KD):
                    pe.wait_ge(ln_sq, sq_at(1))
                    for s in range(2):
                        last = nc.tensor.matmul(bank[4 + s][:, 0:H2], ones, sq[:, k % 4, s * H2:(s + 1) * H2],
                                                start=(k == 0), stop=(k == KD - 1))
                    last.then_inc(sq_used, 1)
                    sq_at.add()

            pe.wait_ge(s_meta, 16)
            for k in range(KD):
                last = nc.tensor.transpose(bank[7][:, k * META:(k + 1) * META], mtok[:, k * P:(k + 1) * P],
                                           ident[0:META, 0:META])
            last.then_inc(meta_done, 1)
            rms2_pe()
            a = (a_hi, a_lo)
            with pe_turns(6, {chunk: 2, tile: 4, fd: 4}):
                for j in range(2):
                    chunk_mm(j, KD, 256, a, fd, banks=(0, 2), n=H2, halves=2, ready=(alo_ready, 6 * KD) if j == 0 else None)
            pe.wait_ge(s_ff, 32)
            for s in range(2):
                for k in range(KD):
                    last = nc.tensor.matmul(bank[4 + s][0:8, 0:H2], wff[:, k, :], xc[:, k, s * H2:(s + 1) * H2],
                                            start=(k == 0), stop=(k == KD - 1))
            last.then_inc(ff_done, 1)
            pe.wait_ge(s_constb, 32)
            pe.wait_ge(free_dve, FD_PROJ)
            pe.wait_ge(fl_ready, 1)
            with pe_turns(2, {b_at: 2}) as i:
                for e, t in enumerate((rq, rk)):
                    pe.wait_ge(r_in, i * 4 + (e + 1))
                    for s in range(2):
                        last = nc.tensor.matmul(bank[2 * e + s][:, 0:H2], rotm, t[:, s * H2:(s + 1) * H2],
                                                start=True, stop=True)
                    last.then_inc(r_rot, 1)
                for e, t in enumerate((rv0, rv1)):
                    pe.wait_ge(r_in, i * 4 + (3 + e))
                    for kb in range(1, 5):
                        nc.tensor.transpose(bank[4 + e][:, (kb - 1) * P:kb * P], t[:, META + (kb - 1) * P:META + kb * P],
                                            ident)
                    nc.tensor.transpose(bank[6][0:META, e * P:(e + 1) * P], t[:, 0:META], ident).then_inc(r_vt, 1)
                for e in range(2):
                    rows = slice(64 * e, 64 * e + 64)

                    def s_mm(kb):
                        k0, nk = key_block(kb)
                        if kb == 0:
                            pe.wait_ge(r_rope, i * 2 + 2)
                            if e:
                                pe.wait_ge(r_rstd, i * 2 + 1)
                            carry(0)
                            for s in range(2):
                                last = nc.tensor.matmul(bank[s][0:META, 0:H2], rk[rows, 0:META],
                                                        rq[rows, s * H2:(s + 1) * H2], start=True, stop=True)
                        else:
                            if kb >= 3:
                                pe.wait_ge(r_sm, i * 10 + (e * 5 + kb - 1))
                            elif e:
                                pe.wait_ge(r_on, i * 4 + 1)
                            last = nc.tensor.matmul(bank[2 + kb % 2][:, 0:L2 - k0], rk[rows, k0:k0 + P],
                                                    rq[rows, k0:L2], start=True, stop=True)
                        last.then_inc(r_s, 1)

                    def o_mm(kb):
                        k0, nk = key_block(kb)
                        pe.wait_ge(r_sm, i * 10 + (e * 5 + kb + 1))
                        for s in range(2):
                            c0, c1 = max(k0, s * H2), (s + 1) * H2
                            if c0 < c1:
                                last = nc.tensor.matmul(bank[4 + 2 * e + s][:, c0 - s * H2:c1 - s * H2],
                                                        rvt[0:nk, kb, e * P:(e + 1) * P], rsm[kb][0:nk, c0 - k0:c1 - k0],
                                                        start=(kb == 0), stop=(kb == 4 or (kb == 2 and s == 0)))
                        return last

                    s_mm(0)
                    s_mm(1)
                    s_mm(2)
                    pe.wait_ge(r_vtok, i * 3 + 3)
                    o_mm(0)
                    s_mm(3)
                    o_mm(1)
                    s_mm(4)
                    o_mm(2)
                    o_mm(3)
                    o_mm(4).then_inc(r_o, 1)
                    pe.wait_ge(r_osq, i * 2 + (e + 1))
                    for s in range(2):
                        last = nc.tensor.matmul(bank[s][:, 0:H2], ones, rsq[:, s * H2:(s + 1) * H2], start=True, stop=True)
                    last.then_inc(r_var, 1)
                    b_at.add()
            pe.wait_ge(ct_ready, 1)
            pe.wait_ge(r_on, 8)
            with pe_turns(4, {b_at: 1}) as i:
                pe.wait_ge(f_in, i * 4 + 4)
                for kb in range(1, 5):
                    nc.tensor.transpose(bank[7][:, (kb - 1) * P:kb * P], fv[:, META + (kb - 1) * P:META + kb * P], ident)
                nc.tensor.transpose(bank[6][0:META, 0:P], fv[:, 0:META], ident).then_inc(f_vt, 1)

                def logits(n):
                    e, qb = n // 5, n % 5
                    q0, q = key_block(qb)
                    rows = slice(64 * e, 64 * e + 64)
                    nk = META + P * qb
                    b = 2 * (n % 2)
                    if n >= 2:
                        pe.wait_ge(f_exp, i * 10 + (n - 1))
                    if qb == 0:
                        carry(b + 1)
                    for k0, k1, dst, bb in ((0, min(nk, 400), 112, b), (400, nk, 0, b + 1)):
                        if k0 < k1:
                            o = bank[bb][0:q, dst:dst + k1 - k0]
                            diag = k1 == nk
                            nc.tensor.matmul(o, fq[rows, q0:q0 + q], fk[rows, k0:k1], start=True, stop=False)
                            last = nc.tensor.matmul(o, sel2[:, e * P:e * P + q], fcs[:, k0:k1], start=False, stop=not diag)
                            if diag:
                                last = nc.tensor.matmul(bank[bb][0:q, dst + k1 - k0 - q:dst + k1 - k0], ident[0:q, 0:q],
                                                        negm[0:q, 0:q], start=False, stop=True)
                    last.then_inc(f_log, 1)

                def turn_p(n):
                    qb = n % 5
                    q = key_block(qb)[1]
                    pe.wait_ge(f_pn, i * 10 + (n + 1))
                    if n:
                        pe.wait_ge(f_pts0, i * 10 + n)
                        if (n - 1) % 5:
                            pe.wait_ge(f_pts, i * 8 + (n - 1) // 5 * 4 + (n - 1) % 5)
                    if qb == 0:
                        carry(4)
                    for kb in range(1, qb + 1):
                        nc.tensor.transpose(bank[4][0:P, (kb - 1) * P:(kb - 1) * P + q],
                                            fp[0:q, n % 2, META + (kb - 1) * P:META + kb * P], ident[0:q, 0:q])
                    nc.tensor.transpose(bank[5][0:META, 0:q], fp[0:q, n % 2, 0:META], ident[0:q, 0:q]).then_inc(f_pt, 1)

                def values(n):
                    e, qb = n // 5, n % 5
                    q = key_block(qb)[1]
                    if n == 0:
                        pe.wait_ge(f_vtok, i * 2 + 2)
                    dst = bank[6][64 * e:64 * e + 64, 0:META] if qb == 0 else \
                        bank[7][64 * e:64 * e + 64, (qb - 1) * P:qb * P]
                    pe.wait_ge(f_pts0, i * 10 + (n + 1))
                    last = nc.tensor.matmul(dst, fvt[0:META, 0, 64 * e:64 * e + 64], fpt0[:, 0:q], start=True, stop=(qb == 0))
                    if qb:
                        pe.wait_ge(f_pts, i * 8 + (e * 4 + qb))
                    for kb in range(1, qb + 1):
                        last = nc.tensor.matmul(dst, fvt[:, kb, 64 * e:64 * e + 64], fpt[:, (kb - 1) * P:kb * P],
                                                start=False, stop=(kb == qb))
                    last.then_inc(f_av, 1)

                logits(0)
                logits(1)
                turn_p(0)
                for n in range(10):
                    if n + 2 < 10:
                        logits(n + 2)
                    if n + 1 < 10:
                        turn_p(n + 1)
                    values(n)
                b_at.add()
            mark = (fa.n, fd.n)
            for j in range(4):
                chunk_mm(j % 2, KD, 256, (b_hi, b_lo), fd, banks=(0, 2), n=H2, halves=2, far=mark if j == 0 else None,
                         ready=(blo_ready, b_at(-KD)) if j == 0 else None)
            rms2_pe()

            def ffn(nt):
                mark = (fa.n, fd.n)
                for j in range(nt):
                    b = 4 * (j % 2)
                    chunk_mm(j % 2, KD, 256, a, (fa, fd), geo=((b, 12, 258, 2), (b + 2, META, T, 1)), far=mark if j == 0 else None,
                             ready=(alo_ready, 7 * KD) if j == 0 else None)
                mark = (fa.n, fd.n)
                for j in range(4):
                    chunk_mm(j % 2, nt, 256, (b_hi, b_lo), fd, far=mark if j < 2 else None, ready=(blo_ready, b_at()) if j == 0 else None)
                b_at.add(nt)

            with pe_turns(2, {chunk: 12, tile: 24, fa: 8, fd: 16, b_at: 8}):
                ffn(8)
            ffn(6)
            rms2_pe()
            pe.wait_ge(xc_ready, 10 * KD)
            for c in range(NCH):
                if c >= 2:
                    pe.wait_ge(ot_ready, 2 * (c - 1))
                for s in range(2):
                    for k in range(4):
                        last = nc.tensor.transpose(bank[2 * (c % 2) + s][:, k * P:(k + 1) * P],
                                                   xc[:, 4 * s + k, META + c * P:META + (c + 1) * P], ident)
                    last.then_inc(ot_done, 1)

        block = ctx.enter_context(nc.Block())

        @block.sync
        def _(sp):
            chunk = Count()

            def load(slot, dst0, src0, dst1, src1):
                sp.wait_ge(wlo_ready, chunk(1))
                sp.dma_start(dst0, src0).then_inc(raw_in[slot], 16)
                sp.dma_start(dst1, src1).then_inc(raw_in[slot], 16)
                chunk.add()

            def load_cols(slot, w, kt, n0, n, k0=0):
                v = raw[:, slot, 0:kt * n].rearrange("p (k n) -> p k n", k=kt)
                h = kt // 2
                load(slot, v[:, 0:h], w[:, bass.ds(k0, h), bass.ds(n0, n)],
                     v[:, h:kt], w[:, bass.ds(k0 + h, kt - h), bass.ds(n0, n)])

            def load_pair(slot, w, na, nb):
                v = raw[:, slot, :].rearrange("p (k n) -> p k n", k=KD)
                load(slot, v[:, :, 0:P], w[:, :, bass.ds(na, P)], v[:, :, P:2 * P], w[:, :, bass.ds(nb, P)])

            def kpn(w):
                return w.rearrange("(k p) n -> p k n", p=P)

            def mlp_loads(layer):
                w1, w2 = kpn(mlp_w1[layer]), kpn(mlp_w2[layer])
                with turns(sp, BLOCKS, {chunk: 8}) as b:
                    for j in range(4):
                        load_cols(j % 2, w1, KD, b * 1024 + j * 256, 256)
                    for j in range(4):
                        load_cols(j % 2, w2, KD, j * 256, 256, k0=b * KD)

            def ple_loads(layer):
                for j in range(4):
                    load_cols(j % 2, kpn(ple_w_gate[layer]), KD, j * 256, 256)
                for j in range(2):
                    load_cols(j % 2, kpn(ple_w_proj[layer]), 2, j * 512, 512)

            for c in range(NCH):
                sp.dma_start(xtok[:, c, :], x[0, c * P:(c + 1) * P, :]).then_inc(s_x, 16)
            sp.dma_start(wdt[:], kpn(ssd_w_in[0])[:, :, 5120:5152]).then_inc(s_wdt, 16)
            w = kpn(ssd_w_in[0])
            wo = kpn(ssd_w_out[0])
            def group(g, final):
                for j in range(2):
                    load_cols(1 - j, w, KD, g * 512 + (DI + j * 256), 256)
                load_cols(1, w, KD, g * P + 2 * DI, P)
                load_cols(0, w, KD, g * P + (2 * DI + 512), P)
                load_cols(1, w, KD, g * 512 + 256, 256)
                if not final:
                    load_cols(0, w, KD, g * 512 + 512, 256)
                for j in range(2):
                    load_cols(j if final else 1 - j, wo, 4, j * 512, 512, k0=g * 4)

            load_cols(0, w, KD, 0, 256)
            with turns(sp, GROUPS - 1, {chunk: 8}) as g:
                group(g, False)
            group(GROUPS - 1, True)
            mlp_loads(0)
            ple_loads(0)
            w = kpn(hgrn_w_in[0])
            for j in range(4):
                load_cols(j % 2, w, KD, 3 * D + j * 256, 256)
            with turns(sp, 8, {chunk: 2}) as h:
                load_pair(0, w, h * P, h * P + D)
                load_cols(1, w, KD, h * P + 2 * D, P)
            for j in range(4):
                load_cols(j % 2, kpn(hgrn_w_out[0]), KD, j * 256, 256)
            mlp_loads(1)
            ple_loads(1)
            block2_sync(sp, chunk, load_cols, load_pair, kpn)

        @block.gpsimd
        def _(pool):
            chunk = Count()
            pub = Count()
            b_at = Count()
            nc.gpsimd.memset(lneps[:, 0:1], LN_EPS)
            nc.gpsimd.memset(lneps[:, 1:2], EPS_2)
            for j, s in enumerate((tile_done, free_act, free_dve)):
                nc.gpsimd.memset(lneps[:, 3 + j:4 + j], 0.0).then_inc(s, BASE)
            nc.gpsimd.memset(lneps[:, 2:3], 0.0).then_inc(wlo_ready, 2)

            def cut_lo(slot, n=2048):
                pool.wait_ge(whi_ready, chunk(1))
                nc.gpsimd.tensor_tensor(w_lo[:, slot, 0:n], raw[:, slot, 0:n],
                                        w_hi[:, slot, 0:n].bitcast(F32), ALU.subtract).then_inc(wlo_ready, 1)
                chunk.add()

            def publish_lo(n0=0, n=T):
                for k in range(KD):
                    pool.wait_ge(ahi_ready, pub(1))
                    nc.gpsimd.tensor_tensor(a_lo[:, k, n0:n0 + n], xc[:, k, n0:n0 + n],
                                            a_hi[:, k, n0:n0 + n].bitcast(F32), ALU.subtract).then_inc(alo_ready, 1)
                    pub.add()

            def ple_lo():
                for k in range(2):
                    pool.wait_ge(bhi_ready, b_at(1))
                    nc.gpsimd.tensor_tensor(b_lo[:, k, 0:T], pf[:, k, :], b_hi[:, k, 0:T].bitcast(F32),
                                            ALU.subtract).then_inc(blo_ready, 1)
                    b_at.add()

            def mlp_lo():
                cuts = (2048,) * 8
                with turns(pool, BLOCKS, {chunk: 8, b_at: KD}):
                    for j, n in enumerate(cuts):
                        cut_lo((j + 1) % 2, n)
                    b_at.add(KD)

            def ple_cuts():
                for j, n in enumerate((2048, 2048, 2048, 1024, 1024, 2048)):
                    cut_lo((j + 1) % 2, n)

            cut_lo(0)
            publish_lo()
            def group(g, final):
                for j, n in enumerate((2048, 1024, 1024, 2048, 2048)):
                    cut_lo(j % 2, n)
                pool.wait_ge(group_ready, g + 1)
                for c in range(3):
                    pool.wait_ge(xdt_ready, g * 4 + (c + 1))
                    if c == 2:
                        pool.wait_ge(st_done, g * 3 + 1)
                    nc.gpsimd.tensor_tensor(
                        xdtd[:, c % 2].rearrange("p (h q) -> p h q", h=HPG),
                        xdt[:, c].rearrange("p (h q) -> p h q", h=HPG),
                        gdte[:, c, :].unsqueeze(2).broadcast_to([P, HPG, 64]), ALU.mult).then_inc(xdtd_ready, 1)
                def gated(j):
                    pool.wait_ge(yv_ready, g * 4 + (j + 1))
                    nc.gpsimd.tensor_tensor(xs[:, j], xs[:, j], zt[:, j], ALU.mult).then_inc(y_ready, 1)

                for r in range(HPG):
                    pool.wait_ge(eh_ready, g * 8 + (r + 1))
                    nc.gpsimd.tensor_tensor(eh[r % 3][:, P:T], eh[r % 3][:, P:T], ct[:, P:T],
                                            ALU.mult).then_inc(ch_ready, 1)
                    if r % 2 == 0 and r:
                        gated(r // 2 - 1)
                gated(3)
                if not final:
                    cut_lo(1)
                for j in range(4):
                    pool.wait_ge(bhi_ready, b_at(1))
                    nc.gpsimd.tensor_tensor(b_lo[:, j, 0:T], xs[:, j], b_hi[:, j, 0:T].bitcast(F32),
                                            ALU.subtract).then_inc(blo_ready, 1)
                    b_at.add()
                for j in range(2):
                    cut_lo(1 - j if final else j)

            cut_lo(1)
            with turns(pool, GROUPS - 1, {chunk: 8, b_at: 4}) as g:
                group(g, False)
            group(GROUPS - 1, True)
            publish_lo()
            mlp_lo()
            ple_lo()
            publish_lo()
            ple_cuts()
            publish_lo()
            hgrn_pool(pool, chunk, b_at, cut_lo)
            publish_lo()
            mlp_lo()
            ple_lo()
            publish_lo()
            ple_cuts()
            block2_pool(pool, chunk, pub, b_at, cut_lo)

        @block.scalar
        def _(act):
            chunk, tile, fa = Count(), Count(BASE), Count(BASE)
            own = Own(act, act_own)
            pub, b_at, ln, sq_at = Count(), Count(), Count(), Count()

            act.dma_start(ident_tri[:], const_a[:, 0:CA_MASK]).then_inc(s_par, 16)
            act.dma_start(prow[0:96, 0, :], ssd_conv_w[0].rearrange("w (t q) -> (w t) q", q=P)).then_inc(s_par, 16)
            act.dma_start(prow[96:120, 0, :], ssd_conv_b[0].rearrange("(t q) -> t q", q=P)).then_inc(s_par, 16)
            row = 0
            for src in (ssd_norm_w[0].rearrange("(t q) -> t q", q=P),
                        ln_g.rearrange("a b (t q) -> (a b t) q", q=P),
                        ln_b.rearrange("a b (t q) -> (a b t) q", q=P),
                        hgrn_norm_w, attn_norm_g[0].rearrange("(t q) -> t q", q=P),
                        ffn_norm_g[0].rearrange("(t q) -> t q", q=P),
                        final_norm_g.rearrange("(t q) -> t q", q=P),
                        ret_norm_g[0].rearrange("(t q) -> t q", q=P)):
                n = src.shape[0]
                act.dma_start(prow[row:row + n, 1, :], src).then_inc(s_par, 16)
                row += n
            act.dma_start(prow[0:3 * F2T, 2, :], conv_w_2[0].rearrange("w (t q) -> (w t) q", q=P)).then_inc(s_par, 16)
            act.dma_start(prow[3 * F2T:4 * F2T, 2, :], conv_b_2[0].rearrange("(t q) -> t q", q=P)).then_inc(s_par, 16)
            act.dma_start(bias32, ssd_dt_bias.broadcast_to([P, HEADS])).then_inc(s_par, 16)
            act.dma_start(nega, ssd_a_log.broadcast_to([P, HEADS])).then_inc(s_par, 16)
            act.dma_start(d32[:], ssd_d.broadcast_to([P, HEADS])).then_inc(s_par, 16)

            act.dma_start(wff[:], w_in_2[0].rearrange("(k q) n -> q k n", q=P)[:, :, 3072:3080]).then_inc(s_ff, 16)
            act.dma_start(fb[:], forget_b.rearrange("a h -> h a")).then_inc(s_ff, 16)

            def cut_hi(slot, n=2048):
                act.wait_ge(raw_in[slot], half(chunk))
                act.wait_ge(tile_done, tile())
                nc.scalar.activation(w_hi[:, slot, 0:n], raw[:, slot, 0:n], ACT.Copy).then_inc(whi_ready, 1)
                chunk.add()

            def half(c):
                if c.iv is None:
                    return 32 * (c.n // 2 + 1)
                assert c.per % 2 == 0
                return c.iv * (16 * c.per) + 32 * (c.n // 2 + 1)

            def publish(scale, n0=0, n=T, write_res=True, r0=0):
                for k in range(KD):
                    act.wait_ge(xc_ready, pub(1))
                    nc.scalar.activation(a_hi[:, k, n0:n0 + n], xc[:, k, n0:n0 + n], ACT.Copy).then_inc(ahi_ready, 1)
                    if write_res:
                        nc.scalar.activation(res[:, k, r0:r0 + n], xc[:, k, n0:n0 + n], ACT.Copy,
                                             scale=scale).then_inc(res_ready, 1)
                    pub.add()

            def ln_act():
                act.preload_act_table_set("natural_log_exp_and_others")
                for k in range(KD):
                    act.wait_ge(ln_xc, ln(k + 1))
                    if sq_at.n or k >= 4:
                        act.wait_ge(sq_used, sq_at(k - 3 if k >= 4 else 0))
                    nc.scalar.activation(sq[:, k % 4, 0:T], xc[:, k, 0:T], ACT.Square).then_inc(ln_sq, 1)
                ln.add(KD)
                sq_at.add(KD)
                act.wait_ge(sq_used, sq_at())
                own.did(nc.scalar.activation(lv[:, 0:T], bank[5], ACT.Ln, scale=1.0 / D, bias=lneps[:, 0:1]))
                own.wait()
                nc.scalar.activation(bank[6], lv[:, 0:T], ACT.Exp, scale=-0.5).then_inc(rstd_ready, 1)

            def mlp_act():
                with turns(act, BLOCKS, {chunk: 8, tile: 16, fa: 8, own.at: 8, b_at: KD}) as b:
                    for j in range(4):
                        cut_hi((j + 1) % 2)
                        for m in range(2):
                            k = 2 * j + m
                            act.wait_ge(tile_done, tile(1))
                            nc.scalar.activation(hu[:, k % 2], bank[tile.n % 4], ACT.Relu).then_inc(free_act, 1)
                            fa.add()
                            act.wait_ge(free_act, fa())
                            act.wait_ge(blo_ready, b_at(-3))
                            own.did(nc.scalar.activation(hv[:, k % 4], hu[:, k % 2], ACT.Square))
                            nc.scalar.activation(b_hi[:, k, 0:T], hu[:, k % 2], ACT.Square).then_inc(bhi_ready, 1)
                            tile.add()
                            b_at.add()
                    for j in range(4):
                        cut_hi((j + 1) % 2)
                        tile.add(2)

            def p_act():
                for k in range(2):
                    act.wait_ge(pt_done, pf_at(k + 1))
                    own.did(nc.scalar.activation(pf[:, k, :], bank[(7, 4)[k]], ACT.Copy))
                    own.wait()
                    nc.scalar.activation(b_hi[:, k, 0:T], bank[(7, 4)[k]], ACT.Copy).then_inc(bhi_ready, 1)
                    b_at.add()
                pf_at.add(2)

            def ple_act():
                for j, n in enumerate((2048, 2048, 2048, 1024, 1024, 2048)):
                    cut_hi((j + 1) % 2, n)
                    if j < 4:
                        for m in range(2):
                            act.wait_ge(tile_done, tile(1))
                            nc.scalar.activation(xc[:, 2 * j + m, 0:T], bank[(2 * j + m) % 4],
                                                 ACT.Sigmoid).then_inc(free_act, 1)
                            fa.add()
                            tile.add()
                    else:
                        tile.add(4)

            pf_at = Count()
            cut_hi(0)
            act.preload_act_table_set("natural_log_exp_and_others")
            act.wait_ge(pcol_done, 1)
            for i, n in enumerate(PROWS):
                nc.scalar.activation(pcol[:, i, 0:n], bank[7][:, i * P:i * P + n], ACT.Copy).then_inc(pcol_ready, 1)
            for s in range(2):
                nc.scalar.activation(dcol[64 * s:64 * s + 64, :], d32[64 * s:64 * s + 64, s::2],
                                     ACT.Copy).then_inc(pcol_ready, 1)
            publish(ALPHA)
            act.wait_ge(dt_tail, 1)
            own.did(nc.scalar.activation(sp1[:], sp0[:], ACT.Abs))
            own.wait()
            own.did(nc.scalar.activation(sp1[:], sp1[:], ACT.Exp, scale=-1.0))
            own.wait()
            own.did(nc.scalar.activation(sp1[:], sp1[:], ACT.Ln, bias=1.0))
            nc.scalar.activation(nega, nega, ACT.Exp).then_inc(da_ready, 1)
            act.wait_ge(dt_tail, 4)
            own.did(nc.scalar.activation(dtep[:, :, :], dtep[:, :, :], ACT.Exp))
            nc.scalar.activation(cdp[:, :, :], bank[5][:, 0:128].rearrange("p (c h) -> p c h", c=NCH),
                                 ACT.Exp).then_inc(da_ready, 1)
            def silu_z(i):
                for m in range(2):
                    act.wait_ge(tile_done, tile(1))
                    nc.scalar.activation(zt[:, i + m], bank[tile.n % 4], ACT.Silu).then_inc(free_act, 1)
                    fa.add()
                    tile.add()

            def group(g, final):
                for j, n in enumerate((2048, 1024, 1024, 2048)):
                    cut_hi(j % 2, n)
                    for m in range(2 if j < 2 else 1):
                        i = 2 * j + m if j < 2 else j + 2
                        dst = xs[:, i] if i < 4 else (bt[:] if i == 4 else ct[:])
                        act.wait_ge(free_dve, g * 14 + (i + 1 + BASE))
                        nc.scalar.activation(dst, dst, ACT.Silu).then_inc(xs_ready, 1)
                        tile.add()
                cut_hi(0)
                silu_z(2)
                act.preload_act_table_set("natural_log_exp_and_others")
                act.wait_ge(bt_done, g + 1)
                nc.scalar.activation(btok[:, :, :], bank[4].rearrange("p (c n) -> p c n", c=NCH),
                                     ACT.Copy).then_inc(bt_ready, 1)
                act.wait_ge(cst_done, g + 1)
                nc.scalar.activation(cst[:], bank[6][0:HPG, :], ACT.Copy).then_inc(cst_ready, 1)

                def y_squares(j):
                    act.wait_ge(y_ready, g * 4 + (j + 1))
                    act.wait_ge(st_done, g * 3 + 3)
                    if j >= 2:
                        act.wait_ge(yvar_done, g * 4 + (j - 1))
                    nc.scalar.activation(xdtd[:, j % 2], xs[:, j], ACT.Square).then_inc(ysq_ready, 1)

                def exp_cs(r):
                    act.wait_ge(csbc_done, g * 8 + (r + 1))
                    if r >= 3:
                        act.wait_ge(y_mm, g * 8 + (r - 2))
                    nc.scalar.activation(eh[r % 3][:, P:T], cs_bank[r % 3][:, P:T], ACT.Exp).then_inc(eh_ready, 1)

                exp_cs(0)
                exp_cs(1)
                for r in range(HPG):
                    act.wait_ge(dm_ready, g * 8 + (r + 1))
                    nc.scalar.activation(em[r % 3], em[r % 3], ACT.Exp).then_inc(em_ready, 1)
                    if r + 2 < HPG:
                        exp_cs(r + 2)
                    if r % 2 == 1 and r >= 3:
                        y_squares(r // 2 - 1)
                y_squares(3)
                if not final:
                    cut_hi(1)
                act.wait_ge(yvar_done, g * 4 + 4)
                own.did(nc.scalar.activation(eh[0], bank[0], ACT.Ln, scale=1.0 / 512, bias=lneps[:, 0:1]))
                own.wait()
                nc.scalar.activation(bank[1], eh[0], ACT.Exp, scale=-0.5).then_inc(yrstd_ready, 1)
                for j in range(4):
                    act.wait_ge(yn_ready, g * 4 + (j + 1))
                    nc.scalar.activation(b_hi[:, j, 0:T], xs[:, j], ACT.Copy).then_inc(bhi_ready, 1)
                    b_at.add()
                if not final:
                    silu_z(0)
                for j in range(2):
                    cut_hi(1 - j if final else j)
                    tile.add(4)

            cut_hi(1)
            silu_z(0)
            with turns(act, GROUPS - 1, {chunk: 8, tile: 18, fa: 4, own.at: 1, b_at: 4}) as g:
                group(g, False)
            group(GROUPS - 1, True)
            def load_p(i):
                act.wait_ge(tile_done, tile())
                act.dma_start(ptok[:], p[i, 0].rearrange("(c q) f -> q c f", q=P)).then_inc(s_ptok, 16)
                if i == 0:
                    act.dma_start(level_masks[:], const_a[:, CA_MASK:CA_W]).then_inc(s_mask, 16)
                else:
                    act.dma_start(mtok[:], meta_tokens).then_inc(s_meta, 16)

            load_p(0)
            ln_act()
            publish(ALPHA)
            mlp_act()
            ln_act()
            p_act()
            publish(1.0)
            ple_act()
            publish(ALPHA)
            hgrn_act(act, chunk, tile, fa, own, b_at, cut_hi)
            load_p(1)
            ln_act()
            publish(ALPHA)
            mlp_act()
            ln_act()
            p_act()
            publish(1.0)
            ple_act()
            block2_act(act, chunk, tile, fa, own, pub, b_at, sq_at, cut_hi)

        @block.vector
        def _(dve):
            tile, fd = Count(BASE), Count(BASE)
            own = Own(dve, dve_own)
            pub, b_at, ln = Count(), Count(), Count()

            def add_to_res(n):
                for m in range(n):
                    dve.wait_ge(tile_done, tile(1))
                    nc.vector.tensor_tensor(res[:, m, 0:T], res[:, m, 0:T], bank[(tile.n) % 4], ALU.add).then_inc(free_dve, 1)
                    tile.add()
                    fd.add()

            def ln_dve(i):
                dve.wait_ge(alo_ready, pub())
                dve.wait_ge(res_ready, res_at())
                dve.wait_ge(mean_done, i + 1)
                for k in range(KD):
                    nc.vector.scalar_tensor_tensor(out=xc[:, k, 0:T], in0=bank[4], scalar=-1.0 / D,
                                                   in1=res[:, k, 0:T], op0=ALU.mult, op1=ALU.add).then_inc(ln_xc, 1)
                ln.add(KD)
                dve.wait_ge(ln_xc, ln())
                dve.wait_ge(rstd_ready, i + 1)
                for k in range(KD + 1):
                    if k < KD:
                        own.did(nc.vector.tensor_tensor(xc[:, k, 0:T], xc[:, k, 0:T], bank[6], ALU.mult))
                    if k >= 1:
                        own.wait(1 if k < KD else 0)
                        nc.vector.tensor_scalar(xc[:, k - 1, 0:T], xc[:, k - 1, 0:T],
                                                col1(C_LG, i * KD + k - 1), col1(C_LB, i * KD + k - 1),
                                                ALU.mult, ALU.add).then_inc(xc_ready, 1)
                pub.add(KD)
                res_at.add(KD)

            def mlp_dve():
                dve.wait_ge(res_ready, res_at())
                with turns(dve, BLOCKS, {tile: 16, fd: 8, b_at: KD}) as b:
                    for k in range(KD):
                        dve.wait_ge(bhi_ready, b_at(1))
                        nc.vector.tensor_tensor(b_lo[:, k, 0:T], hv[:, k % 4], b_hi[:, k, 0:T].bitcast(F32),
                                                ALU.subtract).then_inc(blo_ready, 1)
                        b_at.add()
                        tile.add()
                    add_to_res(8)

            def ple_dve():
                tile.add(8)
                dve.wait_ge(res_ready, res_at())
                for m in range(KD + 1):
                    if m < KD:
                        dve.wait_ge(tile_done, tile(1))
                        nc.vector.tensor_tensor(xc[:, m, 0:T], xc[:, m, 0:T], bank[tile.n % 4],
                                                ALU.mult).then_inc(free_dve, 1)
                        tile.add()
                        fd.add()
                    if m >= 1:
                        dve.wait_ge(free_dve, fd(-1 if m < KD else 0))
                        nc.vector.tensor_tensor(xc[:, m - 1, 0:T], xc[:, m - 1, 0:T], res[:, m - 1, 0:T],
                                                ALU.add).then_inc(xc_ready, 1)
                pub.add(KD)

            res_at = Count()
            for k in range(KD):
                dve.wait_ge(xt_done, k + 1)
                nc.vector.tensor_copy(xc[:, k, 0:T], bank[k % 4]).then_inc(xc_ready, 1)
            pub.add(KD)
            res_at.add(KD)
            dve.wait_ge(s_par, 16 * N_PAR)
            dve.wait_ge(dt_mm, 1)
            nc.vector.tensor_tensor(sp0[:].rearrange("p (c h) -> p c h", c=NCH),
                                    bank[4][:, 0:128].rearrange("p (c h) -> p c h", c=NCH),
                                    bias32.unsqueeze(1).broadcast_to([P, NCH, HEADS]), ALU.add).then_inc(dt_tail, 1)
            dve.wait_ge(da_ready, 1)
            nc.vector.scalar_tensor_tensor(out=small[:, 0:128], in0=sp0[:], scalar=0.0, in1=sp1[:],
                                           op0=ALU.max, op1=ALU.add).then_inc(dt_tail, 1)
            dve.wait_ge(dt_tail, 2)
            nc.vector.scalar_tensor_tensor(out=dap, in0=dtp, scalar=-1.0,
                                           in1=nega.unsqueeze(1).broadcast_to([P, NCH, HEADS]),
                                           op0=ALU.mult, op1=ALU.mult).then_inc(dt_tail, 1)
            dve.wait_ge(cs_mm, 1)
            own.did(nc.vector.tensor_copy(csp[:], bank[6][:, 0:128].rearrange("p (c h) -> p c h", c=NCH)))
            own.wait()
            nc.vector.tensor_tensor(dtep[:], bank[5][:, 0:128].rearrange("p (c h) -> p c h", c=NCH), csp[:],
                                    ALU.subtract).then_inc(dt_tail, 1)
            dve.wait_ge(da_ready, 2)
            dve.wait_ge(pcol_ready, 5)
            xw = pcol[:, 0, 0:120].rearrange("p (w t) -> p w t", w=5)
            def group(g, final):
                dve.wait_ge(tile_done, tile())
                for dst, src in ((gx, xw[:, :, bass.ds(g * 4, 4)]),
                                 (gb.unsqueeze(2), xw[:, :, bass.ds(g + 16, 1)]),
                                 (gc.unsqueeze(2), xw[:, :, bass.ds(g + 20, 1)]),
                                 (gn, pcol[:, 1, bass.ds(g * 4, 4)]), (gd, dcol[:, bass.ds(g * 4, 4)]),
                                 (gdt, dtp[:, :, bass.ds(g * HPG, HPG)]), (gda, dap[:, :, bass.ds(g * HPG, HPG)]),
                                 (gcs, csp[:, :, bass.ds(g * HPG, HPG)]),
                                 (gcd[:], cdp[:, :, bass.ds(g * HPG, HPG)])):
                    nc.vector.tensor_copy(dst, src)
                nc.vector.tensor_copy(gdte, dtep[:, :, bass.ds(g * HPG, HPG)]).then_inc(group_ready, 1)
                dve.wait_ge(group_ready, g + 1)
                for i in range(6):
                    dst = xs[:, i] if i < 4 else (bt[:] if i == 4 else ct[:])
                    tap = [gx[:, w, i:i + 1] if i < 4 else (gb, gc)[i - 4][:, w:w + 1] for w in range(5)]
                    src = bank[tile.n % 4]
                    dve.wait_ge(tile_done, tile(1))
                    own.did(nc.vector.tensor_scalar(dst, src, tap[3], tap[4], ALU.mult, ALU.add))
                    for back in (1, 2):
                        own.wait()
                        own.did(nc.vector.scalar_tensor_tensor(
                            out=dst[:, back:T], in0=src[:, 0:T - back], scalar=tap[3 - back], in1=dst[:, back:T],
                            op0=ALU.mult, op1=ALU.add))
                    own.wait()
                    nc.vector.scalar_tensor_tensor(
                        out=dst[:, 3:T], in0=src[:, 0:T - 3], scalar=tap[0], in1=dst[:, 3:T],
                        op0=ALU.mult, op1=ALU.add).then_inc(free_dve, 1)
                    tile.add()
                    fd.add()
                tile.add(2 if final else 4)
                for c in range(NCH):
                    dve.wait_ge(xtok_done, g * 4 + (c + 1))
                    nc.vector.tensor_tensor(xdt[:, c].rearrange("p (h q) -> p h q", h=HPG),
                                            bank[4 + c].rearrange("p (h q) -> p h q", h=HPG),
                                            gdt[:, c, :].unsqueeze(2).broadcast_to([P, HPG, 64]),
                                            ALU.mult).then_inc(xdt_ready, 1)
                dve.wait_ge(cb_done, g + 1)
                nc.vector.tensor_tensor(cbm[:], bank[5].rearrange("p (c l) -> p c l", c=NCH),
                                        tri.unsqueeze(1).broadcast_to([P, NCH, P]), ALU.mult).then_inc(cbm_ready, 1)
                for c in range(3):
                    dve.wait_ge(st_done, g * 3 + (c + 1))
                    src = bank[6 + c % 2]
                    if c == 0:
                        nc.vector.tensor_copy(hst[:, 0], src).then_inc(hs_ready, 1)
                    else:
                        dve.wait_ge(hs_ready, g * 3 + c)
                        nc.vector.tensor_tensor(
                            hst[:, c].rearrange("p (h q) -> p h q", h=HPG),
                            hst[:, c - 1].rearrange("p (h q) -> p h q", h=HPG),
                            gcd[:, c, :].unsqueeze(2).broadcast_to([P, HPG, 64]), ALU.mult).then_inc(hs_decayed, 1)
                        dve.wait_ge(hs_decayed, g * 2 + c)
                        nc.vector.tensor_tensor(hst[:, c], hst[:, c], src, ALU.add).then_inc(hs_ready, 1)

                def decay(r):
                    dve.wait_ge(eh_ready, g * 8 + (r + 1))
                    if r >= 3:
                        dve.wait_ge(y_mm, g * 8 + (r - 2))
                    for c in range(NCH):
                        last = nc.vector.tensor_scalar(em[r % 3][:, c * P:(c + 1) * P],
                                                       cs_bank[r % 3][:, c * P:(c + 1) * P],
                                                       gcs[:, c, r:r + 1], 0.0, ALU.subtract, ALU.min)
                    last.then_inc(dm_ready, 1)

                def y_tile(j):
                    dve.wait_ge(y_mm, g * 8 + (2 * j + 2))
                    nc.vector.scalar_tensor_tensor(out=xs[:, j], in0=xs[:, j], scalar=gd[:, j:j + 1],
                                                   in1=bank[6 + j % 2], op0=ALU.mult,
                                                   op1=ALU.add).then_inc(yv_ready, 1)

                decay(0)
                decay(1)
                for r in range(HPG):
                    dve.wait_ge(em_ready, g * 8 + (r + 1))
                    nc.vector.tensor_tensor(em[r % 3], em[r % 3], cbm[:].rearrange("p c l -> p (c l)"),
                                            ALU.mult).then_inc(m_ready, 1)
                    if r + 2 < HPG:
                        decay(r + 2)
                    if r % 2 == 0 and r:
                        y_tile(r // 2 - 1)
                y_tile(3)
                dve.wait_ge(yrstd_ready, g + 1)
                for j in range(4):
                    nc.vector.scalar_tensor_tensor(out=xs[:, j], in0=xs[:, j], scalar=gn[:, j:j + 1], in1=bank[1],
                                                   op0=ALU.mult, op1=ALU.mult).then_inc(yn_ready, 1)
                    b_at.add()
                for m in range(8):
                    dve.wait_ge(tile_done, tile(1))
                    if m == 0:
                        dve.wait_ge(res_ready, KD)
                    nc.vector.tensor_tensor(res[:, m, 0:T], res[:, m, 0:T], bank[tile.n % 4],
                                            ALU.add).then_inc(free_dve, 1)
                    tile.add()
                    fd.add()

            tile.add(2)
            with turns(dve, GROUPS - 1, {tile: 18, fd: 14, own.at: 18, b_at: 4}) as g:
                group(g, False)
            group(GROUPS - 1, True)
            ln_dve(0)
            mlp_dve()
            ln_dve(1)
            b_at.add(2)
            ple_dve()
            res_at.add(KD)
            hgrn_dve(dve, tile, fd, own, b_at, add_to_res)
            ln_dve(2)
            mlp_dve()
            ln_dve(3)
            b_at.add(2)
            ple_dve()
            block2_dve(dve, tile, fd, own, pub, b_at)

        @block.tensor
        def _(pe):
            chunk, tile, fa, fd = Count(), Count(BASE), Count(BASE), Count(BASE)
            given_back = {fa: free_act, fd: free_dve}
            last4 = []
            pub, b_at, sq_at = Count(), Count(), Count()

            def chunk_mm(slot, kt, cols, rhs, owner, banks=(0, 4), ready=None, far=None, n0=0, n=T, halves=1,
                         geo=None):
                pe.wait_ge(wlo_ready, chunk(3))
                hi, lo = rhs
                owners = owner if isinstance(owner, tuple) else (owner,)
                wh = w_hi[:, slot, 0:kt * cols].rearrange("p (k n) -> p k n", k=kt)
                wl = w_lo[:, slot, 0:kt * cols].rearrange("p (k n) -> p k n", k=kt)
                for m in range(cols // P):
                    own = owners[m % len(owners)]
                    if far:
                        pe.wait_ge(free_act, fa(far[0] - fa.n))
                        pe.wait_ge(free_dve, fd(far[1] - fd.n))
                    elif geo:
                        pe.wait_ge(given_back[own], own(-1))
                    else:
                        who, n_then = last4[-banks[1]]
                        pe.wait_ge(given_back[who], who(n_then - who.n))
                    if geo:
                        b, c0, nn, hs = geo[m]
                    else:
                        b, c0, nn, hs = banks[0] + (tile.n % banks[1]) * halves, n0, n, halves
                    for k in range(kt):
                        if ready is not None and m == 0:
                            pe.wait_ge(ready[0], ready[1] + (k + 1))
                        for w, v, first, end in ((wh, hi, True, False), (wl, hi, False, False),
                                                 (wh, lo, False, True)):
                            for s in range(hs):
                                last = nc.tensor.matmul(ps[:, b + s, 0:nn], w[:, k, m * P:(m + 1) * P],
                                                        v[:, k, c0 + s * nn:c0 + (s + 1) * nn],
                                                        start=(k == 0 and first), stop=(k == kt - 1 and end))
                    last.then_inc(tile_done, 1)
                    tile.add()
                    own.add()
                    last4[:] = last4[-3:] + [(own, own.n)]
                chunk.add()

            @contextmanager
            def pe_turns(n, counts):
                with turns(pe, n, counts) as iv:
                    yield iv
                last4[:] = [(who, at + (n - 1) * counts.get(who, 0)) for who, at in last4]

            def mlp_pe(alo_from):
                with pe_turns(BLOCKS, {chunk: 8, tile: 16, fa: 8, fd: 8, b_at: KD}):
                    for j in range(4):
                        chunk_mm(j % 2, KD, 256, (a_hi, a_lo), fa, ready=(alo_ready, alo_from) if j == 0 else None)
                    for j in range(4):
                        chunk_mm(j % 2, KD, 256, (b_hi, b_lo), fd, ready=(blo_ready, b_at()) if j == 0 else None)
                    b_at.add(KD)

            def ln_pe():
                for k in range(KD):
                    pe.wait_ge(free_dve, fd(k - 7))
                    last = nc.tensor.matmul(bank[4], ones, res[:, k, 0:T], start=(k == 0), stop=(k == KD - 1))
                last.then_inc(mean_done, 1)
                for k in range(KD):
                    pe.wait_ge(ln_sq, sq_at(1))
                    nc.tensor.matmul(bank[5], ones, sq[:, k % 4, 0:T], start=(k == 0),
                                     stop=(k == KD - 1)).then_inc(sq_used, 1)
                    sq_at.add()

            def p_pe(i):
                pe.wait_ge(s_ptok, 16 * (i + 1))
                for k in range(2):
                    for c in range(NCH):
                        last = nc.tensor.transpose(bank[(7, 4)[k]][:, c * P:(c + 1) * P],
                                                   ptok[:, c, k * P:(k + 1) * P], ident)
                    last.then_inc(pt_done, 1)

            def ple_pe(alo_from):
                for j in range(4):
                    chunk_mm(j % 2, KD, 256, (a_hi, a_lo), fa, ready=(alo_ready, alo_from) if j == 0 else None)
                for j in range(2):
                    chunk_mm(j, 2, 512, (b_hi, b_lo), fd, ready=(blo_ready, b_at()) if j == 0 else None)
                b_at.add(2)

            pe.wait_ge(s_par, 16 * N_PAR)
            for i, n in enumerate(PROWS):
                last = nc.tensor.transpose(bank[7][:, i * P:i * P + n], prow[0:n, i, :], ident[0:n, 0:n])
            last.then_inc(pcol_done, 1)
            pe.wait_ge(s_x, 16 * NCH)
            for k in range(KD):
                if k >= 4:
                    pe.wait_ge(xc_ready, k - 3)
                for c in range(NCH):
                    last = nc.tensor.transpose(bank[k % 4][:, c * P:(c + 1) * P], xtok[:, c, k * P:(k + 1) * P], ident)
                last.then_inc(xt_done, 1)
            pe.wait_ge(xc_ready, KD)
            pe.wait_ge(s_wdt, 16)
            for c in range(NCH):
                for k in range(KD):
                    last = nc.tensor.matmul(bank[4][:, c * HEADS:(c + 1) * HEADS], xc[:, k, c * P:(c + 1) * P],
                                            wdt[:, k, :], start=(k == 0), stop=(k == KD - 1))
            last.then_inc(dt_mm, 1)
            pe.wait_ge(dt_tail, 3)
            nc.tensor.matmul(bank[6][:, 0:P], tri, small[:, 128:256], start=True, stop=True)
            nc.tensor.matmul(bank[5][:, 0:P], ones, small[:, 128:256], start=True, stop=True).then_inc(cs_mm, 1)
            def group(g, final):
                mark = (fa.n, fd.n)
                for j in range(4):
                    chunk_mm(1 - j % 2, KD, 256 if j < 2 else P, (a_hi, a_lo), fd, far=mark if j < 2 else None)
                chunk_mm(1, KD, 256, (a_hi, a_lo), fa)
                for c in range(NCH):
                    for j in range(4):
                        if c == 0:
                            pe.wait_ge(xs_ready, g * 6 + (j + 1))
                        last = nc.tensor.transpose(bank[4 + c][:, j * P:(j + 1) * P], xs[:, j, c * P:(c + 1) * P],
                                                   ident)
                    last.then_inc(xtok_done, 1)
                pe.wait_ge(xs_ready, g * 6 + 6)
                pe.wait_ge(xdt_ready, g * 4 + 1)
                for c in range(NCH):
                    last = nc.tensor.transpose(bank[4][:, c * P:(c + 1) * P], bt[:, c * P:(c + 1) * P], ident)
                last.then_inc(bt_done, 1)
                pe.wait_ge(xdt_ready, g * 4 + 2)
                for c in range(NCH):
                    last = nc.tensor.matmul(bank[5][:, c * P:(c + 1) * P], bt[:, c * P:(c + 1) * P],
                                            ct[:, c * P:(c + 1) * P], start=True, stop=True)
                last.then_inc(cb_done, 1)
                pe.wait_ge(group_ready, g + 1)
                pe.wait_ge(xdt_ready, g * 4 + 3)
                for c in range(NCH):
                    last = nc.tensor.matmul(bank[6][0:HPG, c * P:(c + 1) * P], gda[:, c, :], tri, start=True, stop=True)
                last.then_inc(cst_done, 1)
                pe.wait_ge(bt_ready, g + 1)
                for c in range(3):
                    pe.wait_ge(xdtd_ready, g * 3 + (c + 1))
                    if c == 0:
                        pe.wait_ge(cst_ready, g + 1)
                    if c == 1:
                        pe.wait_ge(xdt_ready, g * 4 + 4)
                    if c == 2:
                        pe.wait_ge(hs_ready, g * 3 + 1)
                    nc.tensor.matmul(bank[6 + c % 2], btok[:, c, :], xdtd[:, c % 2], start=True,
                                     stop=True).then_inc(st_done, 1)

                def bcast(r):
                    if r == 1:
                        pe.wait_ge(cbm_ready, g + 1)
                    if r >= 3:
                        pe.wait_ge(dm_ready, g * 8 + (r - 2))
                        pe.wait_ge(eh_ready, g * 8 + (r - 2))
                    nc.tensor.matmul(cs_bank[r % 3], ident[0:HPG, r:r + 1].broadcast_to([HPG, P]), cst[:],
                                     start=True, stop=True).then_inc(csbc_done, 1)

                def y_sq(j):
                    pe.wait_ge(ysq_ready, g * 4 + (j + 1))
                    nc.tensor.matmul(bank[0], ones, xdtd[:, j % 2], start=(j == 0), stop=(j == 3)).then_inc(yvar_done, 1)

                bcast(0)
                bcast(1)
                for r in range(HPG):
                    if r + 2 < HPG:
                        bcast(r + 2)
                    j, q0 = r // 2, 64 * (r % 2)
                    yb = bank[6 + j % 2]
                    if r == 0:
                        pe.wait_ge(hs_ready, g * 3 + 3)
                    if r % 2 == 0 and j >= 2:
                        pe.wait_ge(yv_ready, g * 4 + (j - 1))
                    pe.wait_ge(m_ready, g * 8 + (r + 1))
                    pe.wait_ge(ch_ready, g * 8 + (r + 1))
                    for c in range(NCH):
                        cols = slice(c * P, (c + 1) * P)
                        last = nc.tensor.matmul(yb[q0:q0 + 64, cols], xdt[:, c, r * 64:(r + 1) * 64],
                                                em[r % 3][:, cols], start=True, stop=(c == 0))
                        if c:
                            last = nc.tensor.matmul(yb[q0:q0 + 64, cols], hst[:, c - 1, r * 64:(r + 1) * 64],
                                                    eh[r % 3][:, cols], start=False, stop=True)
                    last.then_inc(y_mm, 1)
                    if r % 2 == 1 and j >= 2:
                        y_sq(j - 2)
                y_sq(2)
                y_sq(3)
                if not final:
                    chunk_mm(0, KD, 256, (a_hi, a_lo), fa)
                for j in range(2):
                    chunk_mm(j if final else 1 - j, 4, 512, (b_hi, b_lo), fd, ready=(blo_ready, b_at()) if j == 0 else None)
                b_at.add(4)

            chunk_mm(0, KD, 256, (a_hi, a_lo), fa, far=(fa.n, fd.n), ready=(alo_ready, 0))
            with pe_turns(GROUPS - 1, {chunk: 8, tile: 18, fa: 4, fd: 14, b_at: 4}) as g:
                group(g, False)
            group(GROUPS - 1, True)
            ln_pe()
            mlp_pe(KD)
            ln_pe()
            p_pe(0)
            ple_pe(2 * KD)
            hgrn_pe(pe, chunk, tile, fa, fd, pe_turns, b_at, chunk_mm)
            ln_pe()
            mlp_pe(4 * KD)
            ln_pe()
            p_pe(1)
            ple_pe(5 * KD)
            block2_pe(pe, chunk, tile, fa, fd, pe_turns, b_at, chunk_mm, sq_at)


_INS = ["x", "p", "ssd_w_in", "ssd_conv_w", "ssd_conv_b", "ssd_dt_bias", "ssd_a_log", "ssd_d", "ssd_norm_w",
        "ssd_w_out", "hgrn_w_in", "hgrn_norm_w", "hgrn_w_out", "ln_g", "ln_b", "mlp_w1", "mlp_w2",
        "ple_w_proj", "ple_w_gate", "meta_tokens_2", "attn_norm_g_2", "w_in_2", "fox_forget_b_2",
        "ret_norm_g_2", "w_out_2", "ffn_norm_g_2", "w_up_2", "conv_w_2", "conv_b_2", "w_down_2", "final_norm_g_2"]


def kernel(**inputs):
    import concourse.bacc as _bacc
    from concourse.bass_utils import run_bass_kernel_spmd as _run

    nc = _bacc.Bacc("TRN2", target_bir_lowering=False, num_devices=1)
    arrays, args = {}, []
    given = {name: np.ascontiguousarray(inputs[name]) for name in _INS}
    given["const_a"], given["const_b"] = consts_a(), consts_b()
    for name, a in given.items():
        arrays[f"in_{name}_dram"] = a
        args.append(nc.dram_tensor(f"in_{name}_dram", a.shape, F32, kind="ExternalInput").ap())
    out = nc.dram_tensor("out_dram", (1, T, D), F32, kind="ExternalOutput").ap()
    two_blocks(nc, *args, out)
    r = _run(nc, [arrays], core_ids=[0])
    return r.results[0]["out_dram"]
```
